# Optimizing a Trainium2 kernel written in Bass

```python
import math
import jax, jax.numpy as jnp
from jax import lax
import numpy as np

D_MODEL = 1024
BATCH = 1
SEQ = 512
DEPTH = 1
DEC_BATCH = 8
DEC_SEQ = 8
PAST_LEN = 256
PAGE_SIZE = 128

N_HEADS = 8
HEAD_DIM = 64
ATT_WIDTH = N_HEADS * HEAD_DIM
D_SSM = D_MODEL // 2
GROUP_CH = 16
N_GROUPS = D_SSM // GROUP_CH
SSM_STATE = 64
D_FF = 4 * D_MODEL
PLE_DIM = 256
Q_BLOCK = 128
RMS_EPS = 1e-6
DT_MIN = 1e-3
DT_MAX = 1e-1
SB_BIAS_INIT = -6.0
IN_WIDTH = 3 * ATT_WIDTH + D_SSM + 2 * D_MODEL

kernel_name = "hybrid_s5_stickbreaking_decoder_step"

def rms_norm(x, g):
    xf = x.astype(jnp.float32)
    y = xf * lax.rsqrt(jnp.mean(xf * xf, axis=-1, keepdims=True) + RMS_EPS)
    return (y * g.astype(jnp.float32)).astype(x.dtype)

def sb_attend(q, k, v, bias, q_pos):
    scale = HEAD_DIM ** -0.5
    z = (jnp.einsum('bqhd,bkhd->bhqk', q.astype(jnp.float32), k.astype(jnp.float32)) * scale
         + bias.astype(jnp.float32)[None, :, None, None])
    k_pos = jnp.arange(k.shape[1], dtype=jnp.int32)
    mask = k_pos[None, :] < q_pos[:, None]
    log_stay = jnp.where(mask, jax.nn.log_sigmoid(-z), 0.0)
    suffix = lax.cumsum(log_stay, axis=3, reverse=True) - log_stay
    w = jnp.where(mask, jnp.exp(jax.nn.log_sigmoid(z) + suffix), 0.0)
    return jnp.einsum('bhqk,bkhd->bqhd', w, v.astype(jnp.float32)).astype(v.dtype)

def sb_prompt(q, k, v, bias):
    b, s = q.shape[0], q.shape[1]
    nblk = s // Q_BLOCK
    q_blocks = jnp.moveaxis(q.reshape(b, nblk, Q_BLOCK, N_HEADS, HEAD_DIM), 1, 0)
    pos_blocks = jnp.arange(s, dtype=jnp.int32).reshape(nblk, Q_BLOCK)
    o = lax.map(lambda qp: sb_attend(qp[0], k, v, bias, qp[1]), (q_blocks, pos_blocks))
    return jnp.moveaxis(o, 0, 1).reshape(b, s, N_HEADS, HEAD_DIM)

def make_sample_attend(past_k, past_v):
    def attend(q, k, v, bias):
        k_all = jnp.concatenate([past_k, k], axis=1)
        v_all = jnp.concatenate([past_v, v], axis=1)
        q_pos = past_k.shape[1] + jnp.arange(q.shape[1], dtype=jnp.int32)
        return sb_attend(q, k_all, v_all, bias, q_pos)
    return attend

def s5_branch(u, h0, a_re, a_im, log_dt, b_re, b_im, c_re, c_im, d_skip):
    bsz, t = u.shape[0], u.shape[1]
    f32 = jnp.float32
    uf = u.astype(f32)
    ug = uf.reshape(bsz, t, N_GROUPS, GROUP_CH)
    a_re, a_im = a_re.astype(f32), a_im.astype(f32)
    dt = jnp.exp(log_dt.astype(f32))[:, None]
    mag = jnp.exp(a_re * dt)
    ab_re, ab_im = mag * jnp.cos(a_im * dt), mag * jnp.sin(a_im * dt)
    den = a_re * a_re + a_im * a_im
    nr, ni = ab_re - 1.0, ab_im
    f_re = (nr * a_re + ni * a_im) / den
    f_im = (ni * a_re - nr * a_im) / den
    b_re, b_im = b_re.astype(f32), b_im.astype(f32)
    bb_re = f_re[..., None] * b_re - f_im[..., None] * b_im
    bb_im = f_re[..., None] * b_im + f_im[..., None] * b_re
    bu_re = jnp.einsum('btgc,gpc->btgp', ug, bb_re)
    bu_im = jnp.einsum('btgc,gpc->btgp', ug, bb_im)
    h0_re, h0_im = h0[..., 0].astype(f32), h0[..., 1].astype(f32)
    bu_re = bu_re.at[:, 0].add(ab_re * h0_re - ab_im * h0_im)
    bu_im = bu_im.at[:, 0].add(ab_re * h0_im + ab_im * h0_re)
    ar_full = jnp.broadcast_to(ab_re, bu_re.shape)
    ai_full = jnp.broadcast_to(ab_im, bu_im.shape)

    def combine(e1, e2):
        a1r, a1i, b1r, b1i = e1
        a2r, a2i, b2r, b2i = e2
        return (a2r * a1r - a2i * a1i, a2r * a1i + a2i * a1r,
                a2r * b1r - a2i * b1i + b2r, a2r * b1i + a2i * b1r + b2i)

    _, _, hr, hi = lax.associative_scan(combine, (ar_full, ai_full, bu_re, bu_im), axis=1)
    y = (jnp.einsum('btgp,gcp->btgc', hr, c_re.astype(f32))
         - jnp.einsum('btgp,gcp->btgc', hi, c_im.astype(f32)))
    y = y.reshape(bsz, t, D_SSM) + d_skip.astype(f32) * uf
    h_last = jnp.stack([hr[:, -1], hi[:, -1]], axis=-1).astype(h0.dtype)
    return y, h_last

def decoder_layer(x, p_l, h0, attend, g_mix, w_in, g_q, g_k, sb_bias, w_attn_out,
                  a_re, a_im, log_dt, b_re, b_im, c_re, c_im, d_skip,
                  w_glu_val, w_glu_gate, w_out, g_mlp, w_up, w_down, g_ple, w_ple, w_ple_gate):
    b, t = x.shape[0], x.shape[1]
    h = rms_norm(x, g_mix)
    proj = h @ w_in
    q, k, v, u, gate_a, gate_s = jnp.split(
        proj, [ATT_WIDTH, 2 * ATT_WIDTH, 3 * ATT_WIDTH, 3 * ATT_WIDTH + D_SSM,
               3 * ATT_WIDTH + D_SSM + D_MODEL], axis=-1)
    q = rms_norm(q.reshape(b, t, N_HEADS, HEAD_DIM), g_q)
    k = rms_norm(k.reshape(b, t, N_HEADS, HEAD_DIM), g_k)
    v = v.reshape(b, t, N_HEADS, HEAD_DIM)
    o = attend(q, k, v, sb_bias)
    attn_out = o.reshape(b, t, ATT_WIDTH) @ w_attn_out
    y_ssm, h_last = s5_branch(u, h0, a_re, a_im, log_dt, b_re, b_im, c_re, c_im, d_skip)
    y_act = jax.nn.gelu(y_ssm).astype(x.dtype)
    ssm_out = (y_act @ w_glu_val) * jax.nn.sigmoid(y_act @ w_glu_gate)
    merged = jax.nn.sigmoid(gate_a) * attn_out + jax.nn.sigmoid(gate_s) * ssm_out
    x = x + merged @ w_out
    h2 = rms_norm(x, g_mlp)
    x = x + jnp.square(jax.nn.relu(h2 @ w_up)) @ w_down
    h3 = rms_norm(x, g_ple)
    x = x + (p_l @ w_ple) * jax.nn.sigmoid(h3 @ w_ple_gate)
    return x, k, v, h_last

def setup_inputs(seed: int = 0) -> dict:
    key = jax.random.key(seed)
    ks = jax.random.split(key, 40)
    f32 = jnp.float32
    n_pages = PAST_LEN // PAGE_SIZE
    n_used = DEC_BATCH * n_pages
    n_phys = (n_used * 5) // 4

    def nrm(k, shape, scale):
        return jax.random.normal(k, shape, f32) * scale

    page_table = jax.random.permutation(ks[0], n_phys)[:n_used].reshape(DEC_BATCH, n_pages).astype(jnp.int32)
    n_idx = jnp.arange(SSM_STATE, dtype=f32)
    return {
        "x_prompt": nrm(ks[1], (BATCH, SEQ, D_MODEL), 1.0),
        "x_sample": nrm(ks[2], (DEC_BATCH, DEC_SEQ, D_MODEL), 1.0),
        "p_prompt": nrm(ks[3], (DEPTH, BATCH, SEQ, PLE_DIM), 1.0),
        "p_sample": nrm(ks[4], (DEPTH, DEC_BATCH, DEC_SEQ, PLE_DIM), 1.0),
        "cache_k": nrm(ks[5], (DEPTH, n_phys, PAGE_SIZE, N_HEADS, HEAD_DIM), 1.0),
        "cache_v": nrm(ks[6], (DEPTH, n_phys, PAGE_SIZE, N_HEADS, HEAD_DIM), 1.0),
        "state_ssm": nrm(ks[7], (DEPTH, DEC_BATCH, N_GROUPS, SSM_STATE, 2), 0.1),
        "page_table": page_table,
        "g_mix": 1.0 + nrm(ks[8], (DEPTH, D_MODEL), 0.02),
        "w_in": nrm(ks[9], (DEPTH, D_MODEL, IN_WIDTH), D_MODEL ** -0.5),
        "g_q": 1.0 + nrm(ks[10], (DEPTH, HEAD_DIM), 0.02),
        "g_k": 1.0 + nrm(ks[11], (DEPTH, HEAD_DIM), 0.02),
        "sb_bias": SB_BIAS_INIT + nrm(ks[30], (DEPTH, N_HEADS), 0.1),
        "w_attn_out": nrm(ks[12], (DEPTH, ATT_WIDTH, D_MODEL), ATT_WIDTH ** -0.5),
        "ssm_a_re": -0.5 + nrm(ks[13], (DEPTH, N_GROUPS, SSM_STATE), 0.01),
        "ssm_a_im": math.pi * n_idx + nrm(ks[14], (DEPTH, N_GROUPS, SSM_STATE), 0.01),
        "ssm_log_dt": jax.random.uniform(ks[15], (DEPTH, N_GROUPS), f32, math.log(DT_MIN), math.log(DT_MAX)),
        "ssm_b_re": nrm(ks[16], (DEPTH, N_GROUPS, SSM_STATE, GROUP_CH), (2 * GROUP_CH) ** -0.5),
        "ssm_b_im": nrm(ks[17], (DEPTH, N_GROUPS, SSM_STATE, GROUP_CH), (2 * GROUP_CH) ** -0.5),
        "ssm_c_re": nrm(ks[18], (DEPTH, N_GROUPS, GROUP_CH, SSM_STATE), (2 * SSM_STATE) ** -0.5),
        "ssm_c_im": nrm(ks[19], (DEPTH, N_GROUPS, GROUP_CH, SSM_STATE), (2 * SSM_STATE) ** -0.5),
        "ssm_d": nrm(ks[20], (DEPTH, D_SSM), 1.0),
        "w_glu_val": nrm(ks[21], (DEPTH, D_SSM, D_MODEL), D_SSM ** -0.5),
        "w_glu_gate": nrm(ks[22], (DEPTH, D_SSM, D_MODEL), D_SSM ** -0.5),
        "w_out": nrm(ks[23], (DEPTH, D_MODEL, D_MODEL), D_MODEL ** -0.5),
        "g_mlp": 1.0 + nrm(ks[24], (DEPTH, D_MODEL), 0.02),
        "w_up": nrm(ks[25], (DEPTH, D_MODEL, D_FF), D_MODEL ** -0.5),
        "w_down": nrm(ks[26], (DEPTH, D_FF, D_MODEL), D_FF ** -0.5),
        "g_ple": 1.0 + nrm(ks[27], (DEPTH, D_MODEL), 0.02),
        "w_ple": nrm(ks[28], (DEPTH, PLE_DIM, D_MODEL), PLE_DIM ** -0.5),
        "w_ple_gate": nrm(ks[29], (DEPTH, D_MODEL, D_MODEL), D_MODEL ** -0.5),
    }

def reference(x_prompt, x_sample, p_prompt, p_sample, cache_k, cache_v, state_ssm, page_table,
              g_mix, w_in, g_q, g_k, sb_bias, w_attn_out, ssm_a_re, ssm_a_im, ssm_log_dt,
              ssm_b_re, ssm_b_im, ssm_c_re, ssm_c_im, ssm_d, w_glu_val, w_glu_gate, w_out,
              g_mlp, w_up, w_down, g_ple, w_ple, w_ple_gate):
    dec_batch, n_pages = page_table.shape
    past_len = n_pages * cache_k.shape[2]
    xp, xs = x_prompt, x_sample
    h0_prompt = jnp.zeros((x_prompt.shape[0], N_GROUPS, SSM_STATE, 2), state_ssm.dtype)
    kp_l, vp_l, sp_l, ks_l, vs_l, ss_l = [], [], [], [], [], []
    for i in range(DEPTH):
        w = (g_mix[i], w_in[i], g_q[i], g_k[i], sb_bias[i], w_attn_out[i],
             ssm_a_re[i], ssm_a_im[i], ssm_log_dt[i], ssm_b_re[i], ssm_b_im[i],
             ssm_c_re[i], ssm_c_im[i], ssm_d[i], w_glu_val[i], w_glu_gate[i], w_out[i],
             g_mlp[i], w_up[i], w_down[i], g_ple[i], w_ple[i], w_ple_gate[i])
        xp, kp, vp, hp = decoder_layer(xp, p_prompt[i], h0_prompt, sb_prompt, *w)
        past_k = cache_k[i][page_table].reshape(dec_batch, past_len, N_HEADS, HEAD_DIM)
        past_v = cache_v[i][page_table].reshape(dec_batch, past_len, N_HEADS, HEAD_DIM)
        xs, kss, vss, hs = decoder_layer(xs, p_sample[i], state_ssm[i],
                                         make_sample_attend(past_k, past_v), *w)
        kp_l.append(kp); vp_l.append(vp); sp_l.append(hp)
        ks_l.append(kss); vs_l.append(vss); ss_l.append(hs)
    k_prompt = jnp.stack(kp_l); v_prompt = jnp.stack(vp_l); ssm_prompt = jnp.stack(sp_l)
    k_sample = jnp.stack(ks_l); v_sample = jnp.stack(vs_l); ssm_sample = jnp.stack(ss_l)
    return (xp, xs, k_prompt, v_prompt, ssm_prompt, k_sample, v_sample, ssm_sample)


_drawn_inputs = setup_inputs


def setup_inputs(seed=0):
    import zlib

    import numpy as np

    out = dict(_drawn_inputs(seed))
    spreads = {}
    factors = {'g_mix': 2.937,
     'g_q': 8.0,
     'g_k': 2.74,
     'sb_bias': 8.0,
     'ssm_a_re': 15.462,
     'ssm_c_re': 4.375,
     'ssm_c_im': 4.381,
     'g_mlp': 3.348,
     'g_ple': 64.0,
     'cache_k': 8.0,
     'cache_v': 8.0}
    for name, (base, spread) in spreads.items():
        noise = np.random.default_rng([zlib.crc32(name.encode()), seed]).standard_normal(out[name].shape)
        drawn = base * np.exp(spread * noise) if base else spread * noise
        out[name] = __import__('jax').numpy.asarray(drawn.astype(out[name].dtype))
    for name, factor in factors.items():
        out[name] = (out[name] * factor).astype(out[name].dtype)
    return out
```

```python
from contextlib import ExitStack

import numpy as np

import concourse.bass as bass
from concourse import mybir

ALU = mybir.AluOpType
ACT = mybir.ActivationFunctionType
F32 = mybir.dt.float32
F32R = mybir.dt.float32r
I32 = mybir.dt.int32

P = 128
D = 1024
KT = D // P
TP = 512
SB, ST = 8, 8
TS = SB * ST
T = TP + TS
HT = T // 2
H, HD = 8, 64
AW = H * HD
AT = AW // P
NPG, PG = 2, 128
DFF = 4096
PLE = 256
G, GC, NS = 32, 16, 64
GP = G // 2
CH = 8
NCH = T // CH
NPC = TP // CH
EPS = 1e-6
NPAGE, NVNEW = 10, 4
UW = 1024
NRAW, NSPLIT = 5, 3
TOK = [(128 * i, 128) for i in range(4)] + [(TP, TS)]
PI = float(np.pi)
C1 = 6.28125
C2 = float(np.float32(2 * np.pi - C1))
C3 = float(2 * np.pi - C1 - C2)
MAGIC = 12582912.0
ZOFF = {0: 0, 1: 512, 3: 896, 2: 1024}
ZW = 1280
SZW = 3 * 512


def units_of():
    us = [("q", i, 8, 1) for i in range(AT)] + [("k", i, 8, 1) for i in range(AT)]
    us += [("u", i, 8, 1) for i in range(AT)]
    us += [("gate", i, 8, 1) for i in range(9)]
    us += [("v", i, 8, 1) for i in range(AT)]
    us += [("gate", i, 8, 1) for i in range(9, 16)]
    for i in range(4):
        us += [("attn", 2 * i, 4, 2), ("val", 2 * i, 4, 2), ("glu", 2 * i, 4, 2)]
    us += [("out", i, 8, 1) for i in range(KT)]
    us += [("up", i, 8, 1) for i in range(4)]
    for f in range(8):
        for i in range(4):
            if f < 7:
                us.append(("up", 4 * (f + 1) + i, 8, 1))
            us.append(("down", 8 * f + 2 * i, 4, 2))
    us += [("ple", 0, 2, 4), ("ple", 4, 2, 4)]
    us += [("pgate", i, 8, 1) for i in range(KT)]
    return us


DENSE = 4
LASTBANK = 6


def schedule_of(units):
    ev, jobs, uses = [], {}, [0] * 7
    n, dense = [0], [0]

    def job(name, place):
        jobs[name] = (place, uses[place])
        uses[place] += 1

    def dense_job(name):
        job(name, DENSE + dense[0] % 2)
        dense[0] += 1

    def event(*name, place=None):
        ev.append(name)
        if place is not None:
            job(name if len(name) > 1 else name[0], place)

    def unit(k=1):
        for _ in range(k):
            event("unit", n[0])
            for j in range(units[n[0]][3]):
                dense_job(("m", n[0], j))
            n[0] += 1

    event("norm", 0)
    for t in range(5):
        if t < 4:
            event("norm", t + 1)
        for half in range(2):
            event("h", t, half, place=(2 * t + half) % 4)
    event("split0")
    event("s5small")
    event("s5ct", place=2)
    event("s5h0", place=3)
    event("s5big", 0)
    job("qs0", 0)
    job("qs1", 1)
    for p in range(8):
        unit()
        if p:
            event("qksum", p - 1)
    unit()
    event("qksum", 7)
    event("qkrstd")
    unit()
    for p in range(8):
        for half in range(2):
            event("qknorm", p, half, place=half)
    for i in range(4):
        event("gt", 0, i, place=2 + i % 2)
    event("s5big", 1)
    unit(2)
    for i in range(4):
        event("gt", 1, i, place=2 + i % 2)
    for i in range(8):
        event("vs", i, place=2 + i % 2)
        if i < 5:
            event("kout", i, place=i % 2)
    event("vd")
    for q in range(4):
        for half in range(2):
            event("ut", q, half, place=half)
        for half in range(2):
            event("ug", q, half, place=2 + half)
    for i in range(4):
        for part in range(2):
            event("s", i, part, place=2 * (i % 2) + part)
    event("tload")
    for lvl in range(6):
        event("scan", lvl)
        unit((2, 2, 1, 2, 1, 1)[lvl])
    for q in range(4):
        for half in range(2):
            event("y", q, half, place=half)
        for half in range(2):
            event("yt", q, half, place=2 + half)
    event("sfinal", place=0)
    unit(4)
    for t in range(5):
        event("vout", t, place=t % 4)
    jobs["z_before"] = tuple(uses[:6])
    event("pairqk", 0)
    event("z", 0)
    event("z", 1)
    event("pairqk", 1)
    event("lsplit", 0)
    for h in range(H):
        if h % 2 == 0:
            event("pairv", h // 2)
        event("cum", h)
        if h < H - 1:
            event("lsplit", h + 1)
        event("wsplit", h)
        if h + 2 < H:
            event("z", h + 2)
            if h % 2 and h + 3 < H:
                event("pairqk", (h + 3) // 2)
        event("av", h, place=LASTBANK if h % 2 else 3)
    event("sz")
    for j in range(SB * NPG):
        event("skt", j)
        dense_job(("skt", j))
        if j == 7:
            unit()
    event("sl")
    unit(3)
    event("lsplit", H)
    event("scum")
    event("ysplit")
    unit()
    event("sav", place=3)
    event("merge")
    unit(2)
    for i in range(4):
        unit(3)
    for t in range(5):
        for half in range(2):
            event("xT", t, half)
            dense_job(("xT", t, half))
    for m in range(KT):
        unit()
        if m:
            event("ms", 0, m - 1)
    job(("ms", 0, "a"), 0)
    job(("ms", 0, "b"), 1)
    unit()
    event("ms", 0, KT - 1)
    event("msinv", 0)
    unit(3)
    for f in range(7):
        unit(8)
    job(("ms", 1, "a"), 0)
    job(("ms", 1, "b"), 1)
    for t in range(5):
        event("pT", t, place=2 + t % 2)
    for i in range(4):
        unit()
        if i:
            event("ms", 1, 2 * i - 2)
            event("ms", 1, 2 * i - 1)
    unit(2)
    event("ms", 1, 6)
    event("ms", 1, 7)
    event("msinv", 1)
    for m in range(KT + 1):
        if m < KT:
            unit()
        if m:
            event("yout", m - 1)
            job(("yout", m - 1, "a"), 2)
            job(("yout", m - 1, "b"), 3)
    assert n[0] == len(units), (n[0], len(units))
    return ev, jobs


class Count:

    def __init__(self):
        self.made, self.waited, self.last = {}, {}, None

    def up(self, sem):
        self.made[sem] = self.made.get(sem, 0) + 1
        self.last = (sem, self.made[sem])
        return sem

    def upto(self, sem, count):
        self.last = (sem, count)
        return sem

    def next(self, sem):
        self.waited[sem] = self.waited.get(sem, 0) + 1
        return self.waited[sem]


def build(nc, i, o):
    units = units_of()
    schedule, jobs = schedule_of(units)
    ctx = ExitStack()
    with ctx:
        def semaphore(name):
            return ctx.enter_context(nc.semaphore(name))

        def ring(name, slots):
            return [semaphore(f"{name}{slot}") for slot in range(slots)]

        ident_ready = semaphore("ident_ready")
        consts_ready = semaphore("consts_ready")
        gmix_in = semaphore("gmix_in")
        params_in = semaphore("params_in")
        sd_ready = semaphore("sd_ready")
        xn_ready = semaphore("xn_ready")
        h_hi = semaphore("h_hi")
        h_lo = semaphore("h_lo")
        w_hi = semaphore("w_hi")
        w_lo = semaphore("w_lo")
        act_hi = semaphore("act_hi")
        act_lo = semaphore("act_lo")
        sq_ready = semaphore("sq_ready")
        sq_used = semaphore("sq_used")
        nrm_ready = semaphore("nrm_ready")
        dt_ready = semaphore("dt_ready")
        theta_ready = semaphore("theta_ready")
        trig_ready = semaphore("trig_ready")
        s5_powers = semaphore("s5_powers")
        s5_bb = semaphore("s5_bb")
        ca_ready = semaphore("ca_ready")
        gnat_ready = semaphore("gnat_ready")
        vs_ready = semaphore("vs_ready")
        vs_spilled = semaphore("vs_spilled")
        t_in = semaphore("t_in")
        scanned = semaphore("scanned")
        fo_ready = semaphore("fo_ready")
        qk_hi = semaphore("qk_hi")
        qk_lo = semaphore("qk_lo")
        v_hi = semaphore("v_hi")
        v_lo = semaphore("v_lo")
        z_ready = semaphore("z_ready")
        z_abs = semaphore("z_abs")
        l_ready = semaphore("l_ready")
        L_raw = semaphore("L_raw")
        L_masked = semaphore("L_masked")
        L_hi = semaphore("L_hi")
        L_ready = semaphore("L_ready")
        cum_ready = semaphore("cum_ready")
        z_free = semaphore("z_free")
        w_masked = semaphore("w_masked")
        W_hi = semaphore("W_hi")
        w_ready = semaphore("w_ready")
        o_hi = semaphore("o_hi")
        table_in = semaphore("table_in")
        brow_in = semaphore("brow_in")
        qb_ready = semaphore("qb_ready")
        kt_used = semaphore("kt_used")
        vb_used = semaphore("vb_used")
        y_hi = semaphore("y_hi")
        y_lo = semaphore("y_lo")
        gl_sig = semaphore("gl_sig")
        mg_ready = semaphore("mg_ready")
        mg_hi = semaphore("mg_hi")
        mg_lo = semaphore("mg_lo")
        mg_done = semaphore("mg_done")
        xf_ready = semaphore("xf_ready")
        ms_sq = semaphore("ms_sq")
        ms_used = semaphore("ms_used")
        hs_ready = semaphore("hs_ready")
        hid_hi = semaphore("hid_hi")
        hid_lo = semaphore("hid_lo")
        pT_hi = semaphore("pT_hi")
        ysg_ready = semaphore("ysg_ready")
        yf_ready = semaphore("yf_ready")
        stored = semaphore("stored")
        act_steps = semaphore("act_steps")
        dve_steps = semaphore("dve_steps")
        pool_steps = semaphore("pool_steps")
        raw_in = ring("raw_in", NRAW)
        x_in = ring("x_in", 5)
        x2_in = ring("x2_in", 2)
        p_in = ring("p_in", 2)
        page_in = ring("page_in", NPAGE)
        vnew_in = ring("vnew_in", NVNEW)
        gl_in = ring("gl_in", 2)
        gate_out = ring("gate_out", 2)
        k_stored = ring("k_stored", 2)
        psum_full = ring("psum_full", 7)
        psum_free = ring("psum_free", 7)

        def sb(name, shape, dt=F32):
            return ctx.enter_context(nc.sbuf_tensor(name, shape, dt))

        wraw = sb("wraw", [P, NRAW, UW])
        whi = sb("whi", [P, NSPLIT, UW], F32R)
        wlo = sb("wlo", [P, NSPLIT, UW], F32R)
        act = [sb(f"act_{n}", [P, KT, T], F32R) for n in ("hi", "lo")]
        ident = sb("ident", [P, P])
        ones = sb("ones", [P, P])
        tri = sb("tri", [P, P], F32R)
        negs = sb("negs", [P, P], F32R)
        gains = sb("gains", [P, 3, KT])
        gqk = sb("gqk", [P, 2])
        bias = sb("bias", [P, H])
        stat = sb("stat", [P, 3, 5])
        eps = sb("eps", [P, 1])
        halfpi = sb("halfpi", [P, 1])
        hsum = sb("hsum", [P, 8, 16])

        def placed(offset, name, shape, dt=F32):
            with ExitStack() as s:
                if offset:
                    s.enter_context(nc.sbuf_tensor(f"below_{name}", [P, offset // 4], F32))
                return s.enter_context(nc.sbuf_tensor(name, shape, dt))

        yact = placed(0, "yact", [P, AT, T])
        oT = [placed(9216 * (1 + n), f"oT{n}", [P, AT, T], F32R) for n in range(2)]
        qk = placed(27648, "qk", [P, 2, AT, T])
        gst = placed(46080, "gst", [P, 2, T])
        xtok = placed(58880, "xtok", [P, 5, D])
        xsq = placed(58880 + 20480, "xsq", [P, D])
        hf = placed(58880 + 24576, "hf", [P, 2, 4, P])
        gnat = placed(50688, "gnat", [P, GP, CH, GC])
        up_ = placed(50688, "uchunk", [P, 2, 8, CH, GC])
        yb = placed(50688, "ychunk", [P, 2, CH, P])
        tm = [placed(58880 + 9216 * n, f"tm{n}", [P, GP, CH + 1, GC]) for n in range(2)]
        vs = placed(58880, "vs", [GC, G, P])
        UT = placed(58880, "UT", [P, G, NCH])
        uT = placed(0, "uT", [P, AT, T])
        Hb = placed(58880 + 9216, "Hb", [P, 2, GP, NCH])
        sc = [placed(50688, "sc0", [P, 2, GP, NPC - 1]), placed(0, "sc1", [P, 2, GP, NPC - 1])]
        CA = placed(77312, "CA", [P, 2, GP, CH + 1, GC])
        GT = placed(95744, "GT", [P, 2, GP, P])
        Tm = placed(95744, "Tm", [P, G, P])
        at = 112128

        def small(name, shape, dt=F32):
            nonlocal at
            t = placed(at, name, shape, dt)
            at += 4 * int(np.prod(shape[1:]))
            return t

        are, aim, ldt = (small(n, [P, GP]) for n in ("are", "aim", "ldt"))
        ta = [small(f"ta{n}", [P, GP]) for n in range(6)]
        pw_ = small("powers", [P, 2, CH + 1, GP])
        sq8 = small("sq8", [P, 2, 7, GP])
        t9 = [small(f"t9_{n}", [P, 2, GP, 9]) for n in range(2)]
        bnat = placed(0, "bnat", [P, 2, GP, GC])
        bb = small("bb", [P, 2, GP, GC])
        cnat = placed(2048, "cnat", [P, 2, 2, P])
        cT = small("cT", [P, 2, GP, GC])
        h0 = placed(19712, "h0", [P, 2, GP, SB])
        Fh = small("Fh", [P, 2, GP, 9])
        dd = small("dd", [GC, G])
        assert at <= 112128 + 10752, at
        sel = placed(9216, "sel", [16, 8, P])
        kst = placed(13312, "kst", [P, 2, AW])
        nrm = placed(17408, "nrm", [16, T])
        snat = placed(4096, "snat", [P, 2 * P])
        Fo = placed(20736, "Fo", [P, 2, 9 * GP])
        sst = placed(21888, "sst", [P, 2, 2 * P])
        dti = placed(23936, "dti", [GC, G, GC])
        vT = placed(73216, "vT", [P, AT, T])
        vtok = placed(50688, "vtok", [P, 5, AW])
        pr = [placed(60928 + 2048 * n, f"pr{n}", [P, TP], F32R) for n in range(6)]
        khi, klo, qhi, qlo, vhi, vlo = pr
        Lsp, t1, t2 = [], [], []
        for n, (at, w) in enumerate(((73216, SZW), (97792, ZW))):
            Lsp.append([placed(at + 4 * w * q, f"L{n}_{q}", [P, w], F32R) for q in range(2)])
            t1.append(placed(at + 8 * w, f"t1_{n}", [P, w]))
            t2.append(placed(at + 12 * w, f"t2_{n}", [P, w]))
        brow = placed(118272, "brow", [1, SB * AT * 16])
        Qb = placed(120320, "Qb", [P, SB, AT, 16])
        KTb = placed(60928, "KTb", [P, 2, AW])
        vnew = placed(60928 + 4096, "vnew", [ST, NVNEW, AW])
        pages = placed(97792, "pages", [P, NPAGE, AW])
        pti = placed(122368, "pti", [1, SB * NPG], I32)
        sbr = placed(122368 + 64, "sbr", [1, H])
        mg = [placed(46080 + 18432 * n, f"mg{n}", [P, KT, T], F32R) for n in range(2)]
        yh = [placed(27648 + 9216 * n, f"yh{n}", [P, AT, T], F32R) for n in range(2)]
        gl = placed(82944, "gl", [P, 2, 2, 2, T])
        mt = [placed(101376 + 4608 * n, f"mt{n}", [P, 2, T]) for n in range(3)]
        R = placed(0, "R", [P, KT, T])
        xtok2 = placed(115200, "xtok2", [P, 2, D])
        hid = [[placed(64512 + 18432 * b + 9216 * n, f"hid{b}{n}", [P, 4, T], F32R) for n in range(2)] for b in range(2)]
        sq = placed(101376, "sq", [P, 2, T])
        xf = placed(101376 + 4608, "xf", [P, 2, T])
        inv = placed(101376 + 9216, "inv", [P, T])
        hr = placed(101376 + 11520, "hr", [P, 2, T])
        hs = placed(101376 + 16128, "hs", [P, 2, T])
        dtmp = placed(101376 + 20736, "dtmp", [P, 2, T])
        pT = [placed(27648 + 4608 * n, f"pT{n}", [P, 2, T], F32R) for n in range(2)]
        ptok = placed(27648 + 9216, "ptok", [P, 2, PLE])
        pw = placed(27648 + 11264, "pw", [P, KT, T])
        ytok = placed(64512, "ytok", [P, 5, D])
        yf = placed(64512 + 20480, "yf", [P, 2, T])
        ysg = placed(64512 + 20480 + 4608, "ysg", [P, 2, T])

        banks = ctx.enter_context(nc.psum_tensor("banks", [P, 4, 512], F32))
        dense = ctx.enter_context(nc.psum_tensor("dense", [P, 2, 2, 512], F32))
        gates_d = nc.dram_tensor("gates_spill", [16, P, T], F32, kind="Internal").ap()
        vs_d = nc.dram_tensor("vs_spill", [GC, G, P], F32, kind="Internal").ap()

        def bank(job):
            if jobs[job][0] == LASTBANK:
                return dense[:, 1, 1, :]
            return banks[:, jobs[job][0], :]

        def dplace(job):
            return dense[:, jobs[job][0] - DENSE]

        def prod(job):
            return dplace(job)[:, :, 0:HT]

        def halves(ap):
            return ap.rearrange("p (a n) -> p a n", a=2)

        def f32(ap):
            return ap.bitcast(F32)

        def wsrc(u):
            kind, m, nk, nm = units[u]
            name, row, col = {
                "q": ("w_in", 0, 0), "k": ("w_in", 0, AW), "v": ("w_in", 0, 2 * AW), "u": ("w_in", 0, 3 * AW),
                "gate": ("w_in", 0, 4 * AW), "attn": ("w_attn_out", 0, 0), "val": ("w_glu_val", 0, 0),
                "glu": ("w_glu_gate", 0, 0), "out": ("w_out", 0, 0), "up": ("w_up", 0, 0),
                "down": ("w_down", 512 * (m // 8), 0), "ple": ("w_ple", 0, 0), "pgate": ("w_ple_gate", 0, 0)}[kind]
            col += 128 * (m % 8 if kind == "down" else m)
            w = i[name][0][row:row + 128 * nk, col:col + 128 * nm]
            return w.rearrange("(k p) m -> p k m", p=P)

        def wview(t, slot, u):
            return t[:, slot, :].rearrange("p (k m) -> p k m", k=units[u][2])

        def last_job(u):
            return ("m", u, units[u][3] - 1)

        FIRST = {}
        for n, u in enumerate(units):
            FIRST.setdefault(u[0], n)

        def full_of(job):
            return psum_full[jobs[job][0]]

        def free_of(job):
            return psum_free[jobs[job][0]]

        def full(job):
            return full_of(job), jobs[job][1] + 1

        def read(job):
            return free_of(job), jobs[job][1] + 1

        def used_before(job):
            return jobs[job][1] > 0

        def free(job):
            return free_of(job), jobs[job][1]

        block = ctx.enter_context(nc.Block())

        @block.sync
        def _(sync):
            small_loads = [
                (gains[:, 0, :], i["g_mix"][0].rearrange("(k p) -> p k", p=P)),
                (gqk[0:HD, 0:1], i["g_q"].rearrange("a d -> d a")), (gqk[HD:P, 0:1], i["g_q"].rearrange("a d -> d a")),
                (gqk[0:HD, 1:2], i["g_k"].rearrange("a d -> d a")), (gqk[HD:P, 1:2], i["g_k"].rearrange("a d -> d a")),
                (are[:, :], i["ssm_a_re"][0].rearrange("(p g) s -> (g s) p", g=2)),
                (aim[:, :], i["ssm_a_im"][0].rearrange("(p g) s -> (g s) p", g=2)),
                (bnat[:, 0], i["ssm_b_re"][0].rearrange("(p g) s c -> (g s) p c", g=2)),
                (bnat[:, 1], i["ssm_b_im"][0].rearrange("(p g) s c -> (g s) p c", g=2)),
                (snat[:, :], i["state_ssm"][0].rearrange("b (p g) s i -> (b p) (g s i)", g=2)),
                (dd[:, :], i["ssm_d"][0].rearrange("(g c) -> c g", c=GC)),
                (gains[:, 1, :], i["g_mlp"][0].rearrange("(k p) -> p k", p=P)),
                (gains[:, 2, :], i["g_ple"][0].rearrange("(k p) -> p k", p=P)),
                (bias[:, :], i["sb_bias"][0:1, :].to_broadcast([P, H])),
            ]
            for g in range(2):
                small_loads.append((ldt[64 * g:64 * g + 64, :],
                                    i["ssm_log_dt"][0:1].rearrange("a (p g) -> a p g", g=2)[:, :, g].to_broadcast([64, GP])))
                for part, n in enumerate(("ssm_c_re", "ssm_c_im")):
                    for blk in range(2):
                        src = i[n][0][16 * blk:16 * blk + 16].rearrange("(p g) c s -> g p c s", g=2)[g]
                        small_loads.append((cnat[:, part, blk, 64 * g:64 * g + 64], src))

            def weights(u):
                if u >= NRAW:
                    sync.wait_ge(w_lo, u - NRAW + 1)
                dst = wview(wraw, u % NRAW, u)
                sync.dma_start(dst, wsrc(u)).then_inc(raw_in[u % NRAW], 16)

            def tokens(t):
                t0, n = TOK[t]
                src = i["x_prompt"][0][t0:t0 + n, :] if t < 4 else i["x_sample"].rearrange("b s d -> (b s) d")
                sync.dma_start(xtok[0:n, t, :], src).then_inc(x_in[t], 16)

            def load_page(n):
                j, cache = n % (SB * NPG), i["cache_k" if n < SB * NPG else "cache_v"]
                page = sync.value_load(pti[0:1, j:j + 1], min_val=0, max_val=cache.shape[1] - 1)
                sync.dma_start(pages[:, n % NPAGE, :],
                               cache[0][bass.ds(page, 1)].rearrange("a r h d -> (a r) (h d)")).then_inc(page_in[n % NPAGE], 16)

            for t in range(5):
                tokens(t)
            for n, (dst, src) in enumerate(small_loads):
                sync.dma_start(dst, src, allow_slow_non_contiguous=True).then_inc(
                    gmix_in if n == 0 else params_in, 16)
            for u in range(len(units)):
                weights(u)
                if u == FIRST["v"] + AT + 5:
                    sync.wait_ge(table_in, 16)
                    sync.wait_ge(*full(("av", H - 1)))
                    for n in range(SB * NPG + NPAGE):
                        if n >= NPAGE:
                            sync.wait_ge(*full(("skt", n - NPAGE)))
                        load_page(n)
                if u == FIRST["v"] + AT + 9:
                    for n in range(SB * NPG + NPAGE, 2 * SB * NPG):
                        sync.wait_ge(vb_used, (n - SB * NPG - NPAGE) // NPG + 1)
                        load_page(n)

        N_PARAMS = 13 + 2 * 5

        @block.gpsimd
        def _(pool):
            count = Count()
            out_dmas = [0]

            def store(dst, src):
                pool.dma_start(dst, src).then_inc(stored, 16)
                out_dmas[0] += 1

            def tt(out, in0, in1, op):
                return nc.gpsimd.tensor_tensor(out=out, in0=in0, in1=in1, op=op)

            nc.gpsimd.memset(ident[:, :], 0.0).then_inc(count.up(pool_steps), 1)
            nc.gpsimd.memset(ones[:, :], 1.0).then_inc(count.up(pool_steps), 1)
            nc.gpsimd.memset(eps[:, :], EPS).then_inc(count.up(pool_steps), 1)
            nc.gpsimd.memset(halfpi[:, :], PI / 2).then_inc(count.up(pool_steps), 1)
            nc.gpsimd.memset(hsum[:, :, :], 0.0).then_inc(count.up(pool_steps), 1)
            pool.wait_ge(*count.last)
            nc.gpsimd.affine_select(out=ident[:, :], in_=ident[:, :], compare_op=ALU.not_equal, fill=1.0, base=0,
                                   pattern=[[-1, P]], channel_multiplier=1).then_inc(count.up(ident_ready), 1)
            hflat = hsum[:, :, :].rearrange("p a b -> p (a b)")
            pool.wait_ge(*count.last)
            nc.gpsimd.memset(hflat[0:64, 0:P:18], 1.0).then_inc(count.up(pool_steps), 1)
            pool.wait_ge(*count.last)
            nc.gpsimd.memset(hflat[64:P, 1:P:18], 1.0).then_inc(count.up(pool_steps), 1)
            pool.wait_ge(*count.last)
            mneg = gst[:, 0, 0:P]
            nc.gpsimd.memset(mneg, -1.0).then_inc(count.up(pool_steps), 1)
            pool.wait_ge(*count.last)
            nc.gpsimd.tensor_copy(negs[:, :], mneg).then_inc(count.up(pool_steps), 1)
            pool.wait_ge(*count.last)
            nc.gpsimd.affine_select(out=mneg, in_=mneg, compare_op=ALU.is_ge, fill=0.0, base=0,
                                   pattern=[[-1, P]], channel_multiplier=1).then_inc(count.up(pool_steps), 1)
            pool.wait_ge(*count.last)
            nc.gpsimd.tensor_copy(tri[:, :], mneg).then_inc(count.up(pool_steps), 1)
            sflat = sel[:, :, :].rearrange("r p c -> r (p c)")
            nc.gpsimd.memset(sflat, 1.0).then_inc(count.up(pool_steps), 1)
            pool.wait_ge(*count.last)
            nc.gpsimd.affine_select(out=sflat, in_=sflat, compare_op=ALU.is_ge, fill=0.0, base=0,
                                   pattern=[[1, 8 * P]], channel_multiplier=-64).then_inc(count.up(pool_steps), 1)
            pool.wait_ge(*count.last)
            nc.gpsimd.affine_select(out=sflat, in_=sflat, compare_op=ALU.is_ge, fill=0.0, base=63,
                                   pattern=[[-1, 8 * P]], channel_multiplier=64).then_inc(count.up(pool_steps), 1)
            pool.wait_ge(*count.last)
            nc.gpsimd.tensor_copy(stat[:, 2, 0:1], ident[:, 0:1]).then_inc(count.up(consts_ready), 1)

            def powers(lo, hi, n, part, step=1):
                v = pw_[:, part, lo:hi, :].rearrange("q k p -> q p k")
                if step < 0:
                    v = v[:, :, ::-1]
                return v.unsqueeze(3).to_broadcast([P, GP, n, GC])

            def gates_in(j):
                for slot in range(2):
                    pool.wait_ge(gate_out[slot], 16 * (j + 5))
                for which in range(2):
                    src = gates_d[8 * which + 2 * j:8 * which + 2 * j + 2].rearrange("m p t -> p m t")
                    pool.dma_start(gl[:, j % 2, which], src).then_inc(gl_in[j % 2], 16)

            def load_vnew(b):
                pool.dma_start(vnew[:, b % NVNEW, :], vtok[ST * b:ST * b + ST, 4, :]).then_inc(vnew_in[b % NVNEW], 16)

            def load_x2(t):
                t0, n = TOK[t]
                src = i["x_prompt"][0][t0:t0 + n, :] if t < 4 else i["x_sample"].rearrange("b s d -> (b s) d")
                pool.dma_start(xtok2[0:n, t % 2, :], src).then_inc(x2_in[t % 2], 16)

            def load_p(t):
                t0, n = TOK[t]
                src = i["p_prompt"][0, 0][t0:t0 + n, :] if t < 4 else i["p_sample"][0].rearrange("b s d -> (b s) d")
                pool.dma_start(ptok[0:n, t % 2, :], src).then_inc(p_in[t % 2], 16)

            for e in schedule:
                k, a = e[0], e[1:]
                if k == "s5big" and a[0] == 0:
                    pool.wait_ge(s5_powers, 1)
                    pool.wait_ge(h_lo, 10)
                    cr, ci = [cT[:, n].unsqueeze(2).to_broadcast([P, GP, CH + 1, GC]) for n in range(2)]
                    prr, pri = [powers(0, CH + 1, CH + 1, n) for n in range(2)]
                    pool.wait_ge(*read("s5ct"))
                    tt(tm[0][:], prr, cr, ALU.mult).then_inc(count.up(pool_steps), 1)
                    tt(tm[1][:], pri, ci, ALU.mult).then_inc(count.up(pool_steps), 1)
                    pool.wait_ge(*count.last)
                    tt(CA[:, 0], tm[0][:], tm[1][:], ALU.subtract).then_inc(count.up(pool_steps), 1)
                    pool.wait_ge(*count.last)
                    tt(tm[0][:], prr, ci, ALU.mult).then_inc(count.up(pool_steps), 1)
                    tt(tm[1][:], pri, cr, ALU.mult).then_inc(count.up(pool_steps), 1)
                    pool.wait_ge(*count.last)
                    tt(tm[0][:], tm[0][:], tm[1][:], ALU.add).then_inc(count.up(pool_steps), 1)
                    pool.wait_ge(*count.last)
                    nc.gpsimd.tensor_scalar(CA[:, 1], tm[0][:], -1.0, None, ALU.mult).then_inc(count.up(ca_ready), 1)
                    pool.wait_ge(*count.last)
                if k == "s5big":
                    part = a[0]
                    br, bi = [bb[:, n].unsqueeze(2).to_broadcast([P, GP, CH, GC]) for n in range(2)]
                    pr_, pi_ = [powers(0, CH, CH, n, -1) for n in range(2)]
                    if part == 0:
                        pool.wait_ge(s5_bb, 1)
                    else:
                        pool.wait_ge(*full(("gt", 0, 2)))
                        pool.wait_ge(*full(("gt", 0, 3)))
                    tt(tm[0][:, :, 0:CH, :], pr_, br if part == 0 else bi, ALU.mult).then_inc(
                        count.up(pool_steps), 1)
                    tt(tm[1][:, :, 0:CH, :], pi_, bi if part == 0 else br, ALU.mult).then_inc(
                        count.up(pool_steps), 1)
                    pool.wait_ge(*count.last)
                    nc.gpsimd.tensor_tensor(out=gnat[:], in0=tm[0][:, :, 0:CH, :], in1=tm[1][:, :, 0:CH, :],
                                           op=ALU.subtract if part == 0 else ALU.add).then_inc(count.up(gnat_ready), 1)
                elif k == "vd":
                    pool.wait_ge(vs_ready, 1)
                    pool.dma_start(vs_d, vs[:]).then_inc(vs_spilled, 16)
                elif k == "kout":
                    t = a[0]
                    t0, n = TOK[t]
                    pool.wait_ge(*read(("kout", t)))
                    dst = (o["k_prompt"].rearrange("a b s h d -> (a b s) (h d)")[t0:t0 + n, :] if t < 4
                           else o["k_sample"].rearrange("a b s h d -> (a b s) (h d)"))
                    pool.dma_start(dst, kst[0:n, t % 2, :]).then_inc(k_stored[t % 2], 16)
                elif k == "tload":
                    for p in range(2):
                        for n in range(4):
                            pool.wait_ge(*full(("s", n, p)))
                    nc.gpsimd.memset(Tm[:], 0.0).then_inc(count.up(pool_steps), 1)
                    pool.wait_ge(*count.last)
                    pool.wait_ge(vs_spilled, 16)
                    for n in range(CH):
                        pool.dma_start(Tm[GC * n:GC * n + GC, :, GC * n:P],
                                      vs_d[:, :, 0:P - GC * n]).then_inc(t_in, 16)
                elif k == "pairqk" and a[0] == 0:
                    pool.dma_start(pti[:, :], i["page_table"].rearrange("b (n o) -> o (b n)", o=1)).then_inc(table_in, 16)
                elif k == "sfinal":
                    pool.wait_ge(*read("sfinal"))
                    store(o["ssm_sample"].rearrange("a b (p g) s i -> (a b p) (g s i)", g=2), sst[:, 0, :])
                    store(o["ssm_prompt"].rearrange("a b (p g) s i -> (a b p) (g s i)", g=2), sst[0:GP, 1, :])
                elif k == "vout":
                    t = a[0]
                    t0, n = TOK[t]
                    pool.wait_ge(*read(("vout", t)))
                    store(o["v_prompt"].rearrange("a b s h d -> (a b s) (h d)")[t0:t0 + n, :] if t < 4
                          else o["v_sample"].rearrange("a b s h d -> (a b s) (h d)"), vtok[0:n, t, :])
                elif k == "unit" and units[a[0]][0] == "gate":
                    m = units[a[0]][1]
                    pool.wait_ge(*read(("m", a[0], 0)))
                    pool.dma_start(gates_d[m], gst[:, m % 2, :]).then_inc(gate_out[m % 2], 16)
                elif k == "z":
                    pool.wait_ge(L_raw, a[0] + 1)
                    for b in range(4):
                        v = t2[a[0] % 2][:, ZOFF[b]:ZOFF[b] + P]
                        nc.gpsimd.affine_select(out=v, in_=v, compare_op=ALU.is_gt, fill=0.0, base=0,
                                                pattern=[[1, P]], channel_multiplier=-1).then_inc(count.up(L_masked), 1)
                elif k == "cum":
                    pool.wait_ge(z_free, a[0] + 1)
                    for b in range(4):
                        v = t1[a[0] % 2][:, ZOFF[b]:ZOFF[b] + P]
                        nc.gpsimd.affine_select(out=v, in_=v, compare_op=ALU.is_gt, fill=0.0, base=0,
                                                pattern=[[1, P]], channel_multiplier=-1).then_inc(count.up(w_masked), 1)
                elif k == "sz":
                    pool.dma_start(sbr[:, :], i["sb_bias"]).then_inc(brow_in, 16)
                    pool.wait_ge(*full(("av", H - 1)))
                    for b in range(NVNEW):
                        load_vnew(b)
                elif k == "sl":
                    pool.wait_ge(L_raw, H + 1)
                    v = t2[0][0:ST, 1024:SZW].rearrange("p (c t) -> p c t", t=ST)
                    nc.gpsimd.affine_select(out=v, in_=v, compare_op=ALU.is_gt, fill=0.0, base=0,
                                            pattern=[[0, 64], [1, ST]], channel_multiplier=-1).then_inc(count.up(L_masked), 1)
                elif k == "scum":
                    pool.wait_ge(z_free, H + 1)
                    v = t1[0][0:ST, 1024:SZW].rearrange("p (c t) -> p c t", t=ST)
                    nc.gpsimd.affine_select(out=v, in_=v, compare_op=ALU.is_gt, fill=0.0, base=0,
                                            pattern=[[0, 64], [1, ST]], channel_multiplier=-1).then_inc(count.up(w_masked), 1)
                elif k == "sav":
                    for b in range(SB):
                        done = b - NVNEW
                        if done >= 0:
                            pool.wait_ge(vb_used, done + 1)
                            load_vnew(b)
                elif k == "merge":
                    pool.wait_ge(*full("sav"))
                    for j in range(2):
                        gates_in(j)
                    for t in range(2):
                        load_x2(t)
                elif k == "unit" and units[a[0]][0] == "glu":
                    j = units[a[0]][1] // 2
                    if j < 2:
                        pool.wait_ge(mg_done, j + 1)
                        gates_in(j + 2)
                elif k == "xT" and a[1] == 1 and a[0] < 3:
                    pool.wait_ge(*full(("xT", a[0], 1)))
                    load_x2(a[0] + 2)
                elif k == "unit" and units[a[0]][0] == "up" and units[a[0]][1] == 0:
                    pool.wait_ge(*full(("m", a[0] - 1, 0)))
                    for t in range(2):
                        load_p(t)
                elif k == "pT" and a[0] < 3:
                    pool.wait_ge(*full(("pT", a[0])))
                    load_p(a[0] + 2)
                elif k == "yout" and a[0] == KT - 1:
                    pool.wait_ge(*read(("yout", KT - 1, "b")))
                    for t in range(5):
                        t0, n = TOK[t]
                        store(o["y_prompt"][0][t0:t0 + n, :] if t < 4 else o["y_sample"].rearrange("b s d -> (b s) d"),
                              ytok[0:n, t, :])

            pool.wait_ge(k_stored[0], 16 * 3)
            pool.wait_ge(k_stored[1], 16 * 2)
            pool.wait_ge(stored, 16 * out_dmas[0])

        def piece_list(h):
            return [(P, 0, ZW)] if h < H else [(P, 0, 1024), (ST, 1024, SZW)]

        def zflat(h, rows, c0, c1):
            if h % 2:
                return dense[0:rows, :, :, :].rearrange("p a b c -> p (a b c)")[:, c0:c1]
            return banks[0:rows, 0:3, :].rearrange("p b c -> p (b c)")[:, c0:c1]

        def sample_out(h2):
            v = bank("sav").rearrange("q (b p h t) -> q h p b t", b=SB, p=AT, h=2)
            return v[64 * h2:64 * h2 + 64, h2]

        def sample_cols(t, h2):
            return t[64 * h2:64 * h2 + 64, :, TP:T].rearrange("q p (b t) -> q p b t", t=ST)

        @block.scalar
        def _(scalar):
            count = Count()


            def split(u):
                if u >= len(units):
                    return
                scalar.wait_ge(raw_in[u % NRAW], 16 * (u // NRAW + 1))
                if u >= NSPLIT:
                    scalar.wait_ge(*full(last_job(u - NSPLIT)))
                nc.scalar.copy(whi[:, u % NSPLIT, :], wraw[:, u % NRAW, :]).then_inc(count.up(w_hi), 1)

            def feed(m, w):
                scalar.wait_ge(xf_ready, count.next(xf_ready))
                nc.scalar.copy(act[0][:, m, :], xf[:, m % 2, :]).then_inc(count.up(act_hi), 1)
                if m >= 2:
                    scalar.wait_ge(ms_used, (KT - 1) * (w - 1) + m - 1)
                elif w == 2:
                    scalar.wait_ge(*full(("ms", 0, "b")))
                nc.scalar.activation(sq[:, m % 2, :], R[:, m, :], ACT.Square).then_inc(count.up(ms_sq), 1)

            def unit_out(u):
                kind, m0, nk, nm = units[u]
                if kind == "attn":
                    j = m0 // 2
                    scalar.wait_ge(gl_in[j % 2], 32 * (j // 2 + 1))
                    nc.scalar.activation(gl[:, j % 2], gl[:, j % 2], ACT.Sigmoid).then_inc(count.up(gl_sig), 1)
                for j in range(nm):
                    job = ("m", u, j)
                    if kind in ("attn", "val"):
                        continue
                    m = m0 + j
                    if kind in "qk":
                        p = m + (AT if kind == "k" else 0)
                        scalar.wait_ge(*full(job))
                        if p > 1:
                            scalar.wait_ge(sq_used, p - 1)
                        nc.scalar.activation(halves(gst[:, p % 2, :]), prod(job), ACT.Square).then_inc(
                            count.up(sq_ready), 1)
                        nc.scalar.copy(halves(qk[:, p // AT, m, :]), prod(job)).then_inc(count.upto(*read(job)), 1)
                    elif kind == "u":
                        scalar.wait_ge(*full(job))
                        scalar.wait_ge(s5_bb, 1)
                        nc.scalar.copy(halves(uT[:, m, :]), prod(job)).then_inc(count.upto(*read(job)), 1)
                    elif kind == "v":
                        scalar.wait_ge(*full(job))
                        nc.scalar.copy(halves(vT[:, m, :]), prod(job)).then_inc(count.upto(*read(job)), 1)
                    elif kind == "gate":
                        scalar.wait_ge(*full(job))
                        if m > 1:
                            scalar.wait_ge(gate_out[m % 2], 16 * (m // 2))
                        nc.scalar.copy(halves(gst[:, m % 2, :]), prod(job)).then_inc(count.upto(*read(job)), 1)
                    elif kind == "glu":
                        scalar.wait_ge(*full(job))
                        nc.scalar.activation(halves(mt[2][:, j, :]), prod(job), ACT.Sigmoid).then_inc(count.upto(*read(job)), 1)
                    elif kind == "up":
                        scalar.wait_ge(*full(job))
                        nc.scalar.activation(halves(hr[:, m % 2, :]), prod(job), ACT.Relu).then_inc(count.upto(*read(job)), 1)
                        scalar.wait_ge(hs_ready, count.next(hs_ready))
                        nc.scalar.copy(hid[m // 4 % 2][0][:, m % 4, :], hs[:, m % 2, :]).then_inc(count.up(hid_hi), 1)
                    elif kind == "out":
                        feed(m, 1)
                    elif kind == "down" and m0 // 8 == 7:
                        feed(m % 8, 2)
                    elif kind == "ple":
                        scalar.wait_ge(*full(job))
                        nc.scalar.copy(halves(pw[:, m, :]), prod(job)).then_inc(count.upto(*read(job)), 1)
                    elif kind == "pgate":
                        scalar.wait_ge(*read(job))
                        nc.scalar.activation(ysg[:, m % 2, :], yf[:, m % 2, :], ACT.Sigmoid).then_inc(
                            count.up(ysg_ready), 1)
                if kind == "glu":
                    if m0 == 0:
                        for slot in range(2):
                            scalar.wait_ge(gate_out[slot], 16 * 8)
                    for j in range(2):
                        scalar.wait_ge(mg_ready, count.next(mg_ready))
                        nc.scalar.copy(mg[0][:, m0 + j, :], mt[0][:, j, :]).then_inc(count.up(mg_hi), 1)

            for e in schedule:
                k, a = e[0], e[1:]
                if k == "norm":
                    t = a[0]
                    t0, n = TOK[t]
                    scalar.wait_ge(x_in[t], 16)
                    if t:
                        scalar.wait_ge(*count.last)
                    nc.scalar.activation(xsq[0:n, :], xtok[0:n, t, :], ACT.Square,
                                         accum_out=stat[0:n, 0, t:t + 1]).then_inc(count.up(act_steps), 1)
                    scalar.wait_ge(*count.last)
                    if t == 0:
                        scalar.wait_ge(consts_ready, 1)
                    nc.scalar.activation(stat[0:n, 0, t:t + 1], stat[0:n, 0, t:t + 1], ACT.Sqrt, scale=1.0 / D,
                                         bias=eps[0:n, :]).then_inc(count.up(sd_ready), 1)
                elif k == "h":
                    t, half = a
                    t0, n = TOK[t]
                    scalar.wait_ge(*read(("h", t, half)))
                    nc.scalar.copy(act[0][:, 4 * half:4 * half + 4, t0:t0 + n], hf[:, half, :, 0:n]).then_inc(count.up(h_hi), 1)
                elif k == "split0":
                    for u in range(NSPLIT):
                        split(u)
                elif k == "s5small":
                    scalar.wait_ge(params_in, 16 * N_PARAMS)
                    nc.scalar.activation(ta[0][:], ldt[:], ACT.Exp).then_inc(count.up(dt_ready), 1)
                    scalar.wait_ge(theta_ready, 1)
                    nc.scalar.activation(ta[4][:], ta[1][:], ACT.Exp).then_inc(count.up(act_steps), 1)
                    nc.scalar.activation(ta[5][:], ta[2][:], ACT.Sin).then_inc(count.up(act_steps), 1)
                    nc.scalar.activation(ta[0][:], ta[2][:], ACT.Abs).then_inc(count.up(act_steps), 1)
                    scalar.wait_ge(*count.last)
                    nc.scalar.activation(ta[3][:], ta[0][:], ACT.Sin, scale=-1.0, bias=halfpi[:, :]).then_inc(
                        count.up(trig_ready), 1)
                elif k == "unit":
                    unit_out(a[0])
                    split(a[0] + NSPLIT)
                elif k == "qkrstd":
                    for half in range(2):
                        scalar.wait_ge(*full(f"qs{half}"))
                        nc.scalar.activation(nrm[:, HT * half:HT * half + HT], banks[0:16, half, 0:HT], ACT.Sqrt,
                                                 scale=1.0 / HD, bias=eps[0:16, :]).then_inc(count.upto(*read(f"qs{half}")), 1)
                elif k in ("kout", "vout"):
                    t = a[0]
                    t0, n = TOK[t]
                    scalar.wait_ge(*full(e))
                    if k == "kout":
                        if t > 1:
                            scalar.wait_ge(k_stored[t % 2], 16 * (t // 2))
                    dst = kst[0:n, t % 2, :] if k == "kout" else vtok[0:n, t, :]
                    nc.scalar.copy(dst, bank(e)[0:n, :]).then_inc(count.upto(*read(e)), 1)
                elif k == "ut":
                    q, half = a
                    scalar.wait_ge(*full(e))
                    if q >= 2:
                        scalar.wait_ge(*full(("ug", q - 2, 1)))
                    nc.scalar.copy(up_[0:NCH, q % 2, :, 4 * half:4 * half + 4, :].rearrange("n g j c -> n j g c"),
                                       bank(e)[0:NCH, :].rearrange("n (j g c) -> n j g c", j=4, g=8)).then_inc(count.upto(*read(e)), 1)
                elif k == "sfinal":
                    scalar.wait_ge(*full(e[0]))
                    nc.scalar.activation(sst[:, 0, :].rearrange("r (q i) -> r i q", i=2),
                                         banks[:, 0, 0:2 * P].rearrange("r (i q) -> r i q", i=2), ACT.Copy).then_inc(
                        count.up(act_steps), 1)
                    nc.scalar.copy(sst[0:GP, 1, :].rearrange("r (q i) -> r i q", i=2),
                                       banks[0:GP, 0, 2 * P:4 * P].rearrange("r (i q) -> r i q", i=2)).then_inc(count.upto(*read(e[0])), 1)
                elif k == "y":
                    q, half = a
                    scalar.wait_ge(*full(e))
                    if q >= 2:
                        scalar.wait_ge(*full(("yt", q - 2, 1)))
                    nc.scalar.copy(yb[0:NCH, q % 2].rearrange("n j (g c) -> n g j c", c=GC)[:, half::2],
                                       bank(e)[0:NCH, :].rearrange("n (g j c) -> n g j c", g=4, j=CH)).then_inc(count.upto(*read(e)), 1)
                elif k == "yt":
                    q, half = a
                    scalar.wait_ge(*full(e))
                    dst = yact[:, q, :].rearrange("p (n j) -> p j n", j=CH)[:, 4 * half:4 * half + 4, :]
                    nc.scalar.activation(dst, bank(e)[:, 0:4 * NCH].rearrange("p (j n) -> p j n", j=4),
                                             ACT.Gelu_apprx_tanh).then_inc(count.upto(*read(e)), 1)
                elif k == "pairqk":
                    p = a[0]
                    if p:
                        scalar.wait_ge(z_ready, 2 * p)
                    else:
                        scalar.wait_ge(*read(("vout", 3)))
                        scalar.wait_ge(*read(("vout", 4)))
                    nc.scalar.copy(khi[:], qk[:, 1, p, 0:TP]).then_inc(count.up(qk_hi), 1)
                    nc.scalar.copy(qhi[:], qk[:, 0, p, 0:TP]).then_inc(count.up(qk_hi), 1)
                elif k == "pairv":
                    p = a[0]
                    if p:
                        scalar.wait_ge(*full(("av", 2 * p - 1)))
                    nc.scalar.copy(vhi[:].rearrange("s (b c) -> s b c", b=4),
                                   vtok[:, 0:4, P * p:P * p + P]).then_inc(count.up(v_hi), 1)
                elif k in ("z", "sl"):
                    h = a[0] if k == "z" else H
                    t = t1[h % 2]
                    scalar.wait_ge(z_abs, h + 1)
                    for rows, c0, c1 in piece_list(h):
                        nc.scalar.activation(t[0:rows, c0:c1], t[0:rows, c0:c1], ACT.Exp).then_inc(
                            count.up(act_steps), 1)
                    scalar.wait_ge(*count.last)
                    for rows, c0, c1 in piece_list(h):
                        nc.scalar.activation(t[0:rows, c0:c1], t[0:rows, c0:c1], ACT.Ln, bias=1.0).then_inc(
                            count.up(l_ready if c1 > 1024 else act_steps), 1)
                elif k == "lsplit":
                    h = a[0]
                    scalar.wait_ge(L_masked, 4 * h + 4 if h < H else 4 * H + 1)
                    if h >= 2:
                        scalar.wait_ge(*full(("av", h - 2)))
                    for rows, c0, c1 in piece_list(h):
                        nc.scalar.copy(Lsp[h % 2][0][0:rows, c0:c1], t2[h % 2][0:rows, c0:c1]).then_inc(
                            count.up(L_hi if c1 > 1024 else act_steps), 1)
                elif k in ("cum", "scum"):
                    h = a[0] if k == "cum" else H
                    scalar.wait_ge(cum_ready, h + 1)
                    kw = {"bias": bias[:, h:h + 1]} if h < H else {}
                    for rows, c0, c1 in piece_list(h):
                        nc.scalar.activation(t1[h % 2][0:rows, c0:c1], zflat(h, rows, c0, c1), ACT.Exp, **kw).then_inc(
                            count.up(z_free if c1 > 1024 else act_steps), 1)
                elif k == "wsplit":
                    h = a[0]
                    scalar.wait_ge(w_masked, 4 * h + 4)
                    nc.scalar.copy(Lsp[h % 2][0][:, 0:ZW], t1[h % 2][:, 0:ZW]).then_inc(count.up(W_hi), 1)
                elif k == "av":
                    h = a[0]
                    r = 64 * (h % 2)
                    scalar.wait_ge(*full(e))
                    nc.scalar.copy(oT[0][r:r + 64, h // 2, 0:TP], bank(e)[r:r + 64, :]).then_inc(count.up(o_hi), 1)
                elif k == "skt":
                    j = a[0]
                    scalar.wait_ge(*full(e))
                    if j > 1:
                        scalar.wait_ge(kt_used, j - 1)
                    nc.scalar.copy(KTb[:, j % 2, :], dplace(e)[:, 0, :]).then_inc(count.upto(*read(e)), 1)
                elif k == "sav":
                    scalar.wait_ge(*full("sav"))
                    for h2 in range(2):
                        nc.scalar.copy(sample_cols(oT[0], h2), sample_out(h2)).then_inc(count.up(o_hi), 1)
                elif k == "ysplit":
                    nc.scalar.copy(yh[0][:], yact[:]).then_inc(count.up(y_hi), 1)
                elif k == "xT":
                    t, half = a
                    t0, n = TOK[t]
                    scalar.wait_ge(*full(e))
                    nc.scalar.copy(R[:, 4 * half:4 * half + 4, t0:t0 + n],
                                       dplace(e)[:, 0, :].rearrange("p (k n) -> p k n", k=4)[:, :, 0:n]).then_inc(count.upto(*read(e)), 1)
                elif k == "msinv" and a[0] == 1:
                    for half, ab in enumerate("ab"):
                        scalar.wait_ge(*full(("ms", 1, ab)))
                        nc.scalar.activation(inv[:, HT * half:HT * half + HT], banks[:, half, 0:HT], ACT.Sqrt,
                                                 scale=1.0 / D, bias=eps[:, :]).then_inc(count.upto(*read(("ms", 1, ab))), 1)
                elif k == "pT":
                    t = a[0]
                    t0, n = TOK[t]
                    scalar.wait_ge(*full(e))
                    nc.scalar.copy(pT[0][:, :, t0:t0 + n], bank(e)[:, 0:2 * P].rearrange("p (k n) -> p k n", k=2)[:, :, 0:n]).then_inc(count.up(pT_hi), 1)
                elif k == "yout":
                    m = a[0]
                    scalar.wait_ge(*full(("yout", m, "a")))
                    nc.scalar.copy(ytok[:, 0:4, P * m:P * m + P], banks[:, 2, :].rearrange("p (t c) -> p t c", t=4)).then_inc(count.upto(*read(("yout", m, "a"))), 1)
                    scalar.wait_ge(*full(("yout", m, "b")))
                    nc.scalar.copy(ytok[0:TS, 4, P * m:P * m + P], banks[0:TS, 3, 0:P]).then_inc(count.upto(*read(("yout", m, "b"))), 1)

        @block.vector
        def _(vector):
            count = Count()

            def tt(out, in0, in1, op):
                return nc.vector.tensor_tensor(out=out, in0=in0, in1=in1, op=op)

            def cmul(out_re, out_im, a_re, a_im, b_re, b_im, s1, s2):
                tt(out=s1, in0=a_re, in1=b_re, op=ALU.mult).then_inc(count.up(dve_steps), 1)
                tt(out=s2, in0=a_im, in1=b_im, op=ALU.mult).then_inc(count.up(dve_steps), 1)
                vector.wait_ge(*count.last)
                tt(out=out_re, in0=s1, in1=s2, op=ALU.subtract).then_inc(count.up(dve_steps), 1)
                vector.wait_ge(*count.last)
                tt(out=s1, in0=a_re, in1=b_im, op=ALU.mult).then_inc(count.up(dve_steps), 1)
                tt(out=s2, in0=a_im, in1=b_re, op=ALU.mult).then_inc(count.up(dve_steps), 1)
                vector.wait_ge(*count.last)
                tt(out=out_im, in0=s1, in1=s2, op=ALU.add).then_inc(count.up(dve_steps), 1)
                vector.wait_ge(*count.last)

            def lower(lo, whole, hi):
                return nc.vector.tensor_tensor(out=lo, in0=whole, in1=f32(hi), op=ALU.subtract)

            def split(u):
                if u < len(units):
                    vector.wait_ge(w_hi, u + 1)
                    lower(wlo[:, u % NSPLIT, :], wraw[:, u % NRAW, :], whi[:, u % NSPLIT, :]).then_inc(
                        count.up(w_lo), 1)

            def feed(m, w):
                vector.wait_ge(*count.last)
                nc.vector.tensor_scalar(xf[:, m % 2, :], R[:, m, :], gains[:, w, m:m + 1], None, ALU.mult).then_inc(count.up(xf_ready), 1)
                vector.wait_ge(act_hi, KT * (w - 1) + m + 1)
                lower(act[1][:, m, :], xf[:, m % 2, :], act[0][:, m, :]).then_inc(count.up(act_lo), 1)

            def unit_out(u):
                kind, m0, nk, nm = units[u]
                for j in range(nm):
                    job = ("m", u, j)
                    m = m0 + j
                    if kind == "attn":
                        if j == 0:
                            vector.wait_ge(gl_sig, count.next(gl_sig))
                            if m == 0:
                                vector.wait_ge(stored, 16 * 7)
                        vector.wait_ge(*full(job))
                        nc.vector.tensor_tensor(out=halves(mt[0][:, j, :]), in0=halves(gl[:, m0 // 2 % 2, 0, j, :]),
                                                   in1=prod(job), op=ALU.mult).then_inc(count.upto(*read(job)), 1)
                    elif kind == "val":
                        vector.wait_ge(*full(job))
                        nc.vector.tensor_tensor(out=halves(mt[1][:, j, :]), in0=halves(gl[:, m0 // 2 % 2, 1, j, :]),
                                                   in1=prod(job), op=ALU.mult).then_inc(count.upto(*read(job)), 1)
                    elif kind == "glu":
                        vector.wait_ge(*read(job))
                        vector.wait_ge(*count.last)
                        tt(mt[1][:, j, :], mt[1][:, j, :], mt[2][:, j, :], ALU.mult).then_inc(
                            count.up(dve_steps), 1)
                        vector.wait_ge(*count.last)
                        tt(mt[0][:, j, :], mt[0][:, j, :], mt[1][:, j, :], ALU.add).then_inc(
                            count.up(mg_ready), 1)
                    elif kind == "up":
                        vector.wait_ge(*read(job))
                        tt(hs[:, m % 2, :], hr[:, m % 2, :], hr[:, m % 2, :], ALU.mult).then_inc(
                            count.up(hs_ready), 1)
                        vector.wait_ge(hid_hi, m + 1)
                        b = m // 4 % 2
                        lower(hid[b][1][:, m % 4, :], hs[:, m % 2, :], hid[b][0][:, m % 4, :]).then_inc(
                            count.up(hid_lo), 1)
                    elif kind == "out":
                        vector.wait_ge(*full(job))
                        nc.vector.tensor_tensor(out=halves(R[:, m, :]), in0=halves(R[:, m, :]), in1=prod(job),
                                                   op=ALU.add).then_inc(count.upto(*read(job)), 1)
                        feed(m, 1)
                    elif kind == "down":
                        vector.wait_ge(*full(job))
                        nc.vector.tensor_tensor(out=halves(dtmp[:, m % 2, :]), in0=halves(inv[:]), in1=prod(job),
                                                   op=ALU.mult).then_inc(count.upto(*read(job)), 1)
                        vector.wait_ge(*count.last)
                        tt(R[:, m % 8, :], R[:, m % 8, :], dtmp[:, m % 2, :], ALU.add).then_inc(
                            count.up(dve_steps), 1)
                        if m0 // 8 == 7:
                            feed(m % 8, 2)
                    elif kind == "pgate":
                        vector.wait_ge(*full(job))
                        if m >= 2:
                            vector.wait_ge(*full(("yout", m - 2, "b")))
                        nc.vector.tensor_tensor(out=halves(yf[:, m % 2, :]), in0=halves(inv[:]), in1=prod(job),
                                                   op=ALU.mult).then_inc(count.upto(*read(job)), 1)
                        vector.wait_ge(ysg_ready, count.next(ysg_ready))
                        tt(yf[:, m % 2, :], ysg[:, m % 2, :], pw[:, m, :], ALU.mult).then_inc(
                            count.up(dve_steps), 1)
                        vector.wait_ge(*count.last)
                        tt(yf[:, m % 2, :], yf[:, m % 2, :], R[:, m, :], ALU.add).then_inc(count.up(yf_ready), 1)
                if kind == "glu":
                    for j in range(2):
                        vector.wait_ge(mg_hi, count.next(mg_hi))
                        lower(mg[1][:, m0 + j, :], mt[0][:, j, :], mg[0][:, m0 + j, :]).then_inc(
                            count.up(mg_lo), 1)
                    tt(stat[:, 1, 0:1], eps[:, :], eps[:, :], ALU.add).then_inc(count.up(mg_done), 1)
                    vector.wait_ge(*count.last)

            vector.wait_ge(gmix_in, 16)
            for e in schedule:
                k, a = e[0], e[1:]
                if k == "norm":
                    t = a[0]
                    n = TOK[t][1]
                    vector.wait_ge(sd_ready, t + 1)
                    nc.vector.reciprocal(stat[0:n, 1, t:t + 1], stat[0:n, 0, t:t + 1]).then_inc(count.up(dve_steps), 1)
                    vector.wait_ge(*count.last)
                    nc.vector.tensor_scalar(xtok[0:n, t, :], xtok[0:n, t, :], stat[0:n, 1, t:t + 1], None,
                                            ALU.mult).then_inc(count.up(xn_ready), 1)
                elif k == "h":
                    t, half = a
                    t0, n = TOK[t]
                    vector.wait_ge(*full(e))
                    nc.vector.tensor_tensor(out=hf[:, half, :, 0:n],
                                               in0=gains[:, 0, 4 * half:4 * half + 4].unsqueeze(2).to_broadcast([P, 4, n]),
                                               in1=bank(e).rearrange("p (k n) -> p k n", k=4)[:, :, 0:n], op=ALU.mult).then_inc(count.upto(*read(e)), 1)
                    vector.wait_ge(h_hi, count.next(h_hi))
                    lower(act[1][:, 4 * half:4 * half + 4, t0:t0 + n], hf[:, half, :, 0:n],
                          act[0][:, 4 * half:4 * half + 4, t0:t0 + n]).then_inc(count.up(h_lo), 1)
                elif k == "split0":
                    for u in range(NSPLIT):
                        split(u)
                elif k == "s5small":
                    vector.wait_ge(params_in, 16 * N_PARAMS)
                    nc.vector.tensor_scalar(gqk[:, 0:1], gqk[:, 0:1], HD ** -0.5, None, ALU.mult).then_inc(count.up(dve_steps), 1)
                    nc.vector.memset(pw_[:, 0, 0, :], 1.0).then_inc(count.up(dve_steps), 1)
                    nc.vector.memset(pw_[:, 1, 0, :], 0.0).then_inc(count.up(dve_steps), 1)
                    vector.wait_ge(dt_ready, 1)
                    tt(ta[1][:], are[:], ta[0][:], ALU.mult).then_inc(count.up(dve_steps), 1)
                    tt(ta[2][:], aim[:], ta[0][:], ALU.mult).then_inc(count.up(dve_steps), 1)
                    vector.wait_ge(*count.last)
                    nc.vector.tensor_scalar(ta[3][:], ta[2][:], 1.0 / (2 * PI), MAGIC, ALU.mult, ALU.add).then_inc(count.up(dve_steps), 1)
                    vector.wait_ge(*count.last)
                    nc.vector.tensor_scalar(ta[3][:], ta[3][:], MAGIC, None, ALU.subtract).then_inc(count.up(dve_steps), 1)
                    vector.wait_ge(*count.last)
                    for c in (C1, C2, C3):
                        nc.vector.scalar_tensor_tensor(out=ta[2][:], in0=ta[3][:], scalar=-c, in1=ta[2][:],
                                                      op0=ALU.mult, op1=ALU.add).then_inc(count.up(dve_steps), 1)
                        vector.wait_ge(*count.last)
                    lim = 3.1415925
                    nc.vector.tensor_scalar(ta[2][:], ta[2][:], lim, -lim, ALU.min, ALU.max).then_inc(count.up(theta_ready), 1)
                    vector.wait_ge(trig_ready, 1)
                    tt(pw_[:, 0, 1, :], ta[4][:], ta[3][:], ALU.mult).then_inc(count.up(dve_steps), 1)
                    tt(pw_[:, 1, 1, :], ta[4][:], ta[5][:], ALU.mult).then_inc(count.up(dve_steps), 1)
                    vector.wait_ge(*count.last)
                    for n in (1, 2, 4):
                        an = [pw_[:, q, n, :].unsqueeze(1).to_broadcast([P, n, GP]) for q in range(2)]
                        dst = [pw_[:, q, n + 1:2 * n + 1, :] for q in range(2)]
                        src = [pw_[:, q, 1:n + 1, :] for q in range(2)]
                        s1, s2 = [t9[q][:].rearrange("p a b c -> p (a b c)")[:, 0:n * GP].rearrange("p (n g) -> p n g", g=GP)
                                  for q in range(2)]
                        cmul(dst[0], dst[1], src[0], src[1], an[0], an[1], s1, s2)
                    for q in range(2):
                        nc.vector.tensor_copy(sq8[:, q, 0, :], pw_[:, q, 8, :]).then_inc(count.up(dve_steps), 1)
                    vector.wait_ge(*count.last)
                    for n in range(5):
                        c = [sq8[:, q, n, :] for q in range(2)]
                        cmul(sq8[:, 0, n + 1, :], sq8[:, 1, n + 1, :], c[0], c[1], c[0], c[1],
                             ta[0][:], ta[1][:])
                    nc.vector.tensor_scalar(ta[2][:], pw_[:, 0, 1, :], -1.0, None, ALU.add).then_inc(count.up(s5_powers), 1)
                    tt(ta[0][:], are[:], are[:], ALU.mult).then_inc(count.up(dve_steps), 1)
                    tt(ta[1][:], aim[:], aim[:], ALU.mult).then_inc(count.up(dve_steps), 1)
                    vector.wait_ge(*count.last)
                    tt(ta[0][:], ta[0][:], ta[1][:], ALU.add).then_inc(count.up(dve_steps), 1)
                    vector.wait_ge(*count.last)
                    nc.vector.reciprocal(ta[0][:], ta[0][:]).then_inc(count.up(dve_steps), 1)
                    tt(ta[3][:], ta[2][:], are[:], ALU.mult).then_inc(count.up(dve_steps), 1)
                    tt(ta[4][:], pw_[:, 1, 1, :], aim[:], ALU.mult).then_inc(count.up(dve_steps), 1)
                    vector.wait_ge(*count.last)
                    tt(ta[3][:], ta[3][:], ta[4][:], ALU.add).then_inc(count.up(dve_steps), 1)
                    vector.wait_ge(*count.last)
                    tt(ta[4][:], pw_[:, 1, 1, :], are[:], ALU.mult).then_inc(count.up(dve_steps), 1)
                    tt(ta[5][:], ta[2][:], aim[:], ALU.mult).then_inc(count.up(dve_steps), 1)
                    vector.wait_ge(*count.last)
                    tt(ta[4][:], ta[4][:], ta[5][:], ALU.subtract).then_inc(count.up(dve_steps), 1)
                    vector.wait_ge(*count.last)
                    tt(ta[3][:], ta[3][:], ta[0][:], ALU.mult).then_inc(count.up(dve_steps), 1)
                    tt(ta[4][:], ta[4][:], ta[0][:], ALU.mult).then_inc(count.up(dve_steps), 1)
                    vector.wait_ge(*count.last)
                    f = [ta[3 + q][:].unsqueeze(2).to_broadcast([P, GP, GC]) for q in range(2)]
                    s1, s2 = [t9[q][:].rearrange("p a b c -> p (a b c)")[:, 0:GP * GC].rearrange("p (a c) -> p a c", c=GC)
                              for q in range(2)]
                    cmul(bb[:, 0], bb[:, 1], f[0], f[1], bnat[:, 0], bnat[:, 1], s1, s2)
                    nc.vector.memset(stat[:, 2, 1:2], 0.0).then_inc(count.up(s5_bb), 1)
                elif k == "s5ct":
                    vector.wait_ge(*full("s5ct"))
                    nc.vector.tensor_copy(cT[:].rearrange("p a b c -> p (a b c)"), bank("s5ct")).then_inc(count.upto(*read("s5ct")), 1)
                elif k == "s5h0":
                    vector.wait_ge(*full("s5h0"))
                    nc.vector.tensor_copy(h0[:], bank("s5h0")[:, 0:2 * P].rearrange("q (i b p) -> q i p b", i=2, b=SB)).then_inc(count.upto(*read("s5h0")), 1)
                elif k == "unit":
                    unit_out(a[0])
                    split(a[0] + NSPLIT)
                elif k == "qkrstd":
                    vector.wait_ge(*read("qs0"))
                    vector.wait_ge(*read("qs1"))
                    nc.vector.reciprocal(nrm[:], nrm[:]).then_inc(count.up(nrm_ready), 1)
                elif k == "qknorm":
                    p, half = a
                    vector.wait_ge(*full(e))
                    x = qk[:, p // AT, p % AT, HT * half:HT * half + HT]
                    nc.vector.scalar_tensor_tensor(out=x, in0=x, scalar=gqk[:, p // AT:p // AT + 1],
                                                      in1=bank(e)[:, 0:HT], op0=ALU.mult, op1=ALU.mult).then_inc(count.upto(*read(e)), 1)
                elif k == "gt":
                    part, n = a
                    vector.wait_ge(*full(e))
                    nc.vector.tensor_copy(GT[:, part, 4 * n:4 * n + 4, :].rearrange("p a b -> p (a b)"), bank(e)).then_inc(count.upto(*read(e)), 1)
                elif k == "vs":
                    vector.wait_ge(*full(e))
                    vector.wait_ge(gnat_ready, 2)
                    g0 = 8 * (a[0] // 2)
                    nc.vector.tensor_copy(vs[:, g0 + a[0] % 2:g0 + 8:2, :],
                                             bank(e)[0:GC, :].rearrange("p (a b) -> p a b", a=4)).then_inc(count.upto(*read(e)), 1)
                elif k == "vd":
                    tt(dti[:], ident[0:GC, 0:GC].unsqueeze(1).to_broadcast([GC, G, GC]),
                       dd[:].unsqueeze(2).to_broadcast([GC, G, GC]), ALU.mult).then_inc(count.up(dve_steps), 1)
                    vector.wait_ge(*count.last)
                    tt(vs[:, :, 0:GC], vs[:, :, 0:GC], dti[:], ALU.add).then_inc(count.up(vs_ready), 1)
                elif k == "ug":
                    q, half = a
                    vector.wait_ge(*full(e))
                    vector.wait_ge(vs_spilled, 16)
                    nc.vector.tensor_copy(UT[:, 8 * q + 4 * half:8 * q + 4 * half + 4, :].rearrange("p g n -> p (g n)"),
                                             bank(e)[:, 0:4 * NCH]).then_inc(count.upto(*read(e)), 1)
                elif k == "s":
                    n, part = a
                    vector.wait_ge(*full(e))
                    if n == 0 and part == 0:
                        nc.vector.memset(Hb[:, :, :, 0:1], 0.0).then_inc(count.up(dve_steps), 1)
                        nc.vector.tensor_copy(Hb[:, :, :, NPC:NCH], h0[:]).then_inc(count.up(dve_steps), 1)
                    src = bank(e)[:, 0:4 * NCH].rearrange("p (a n) -> p a n", a=4)
                    nc.vector.tensor_copy(Hb[:, part, 4 * n:4 * n + 4, 1:NPC], src[:, :, 0:NPC - 1]).then_inc(count.up(dve_steps), 1)
                    nc.vector.tensor_copy(Fh[:, part, 4 * n:4 * n + 4, :], src[:, :, NPC - 1:NCH]).then_inc(count.upto(*read(e)), 1)
                elif k == "scan":
                    lvl = a[0]
                    d = 1 << lvl
                    n = NPC - 1 - d
                    vector.wait_ge(*count.last)
                    src = Hb[:, :, :, 1:1 + n]
                    for q in range(2):
                        c = sq8[:, q, lvl, :].unsqueeze(1).unsqueeze(3).to_broadcast([P, 2, GP, n])
                        tt(sc[q][:, :, :, 0:n], src, c, ALU.mult).then_inc(count.up(dve_steps), 1)
                    vector.wait_ge(*count.last)
                    dst = Hb[:, :, :, 1 + d:NPC]
                    tt(dst, dst, sc[0][:, :, :, 0:n], ALU.add).then_inc(count.up(dve_steps), 1)
                    vector.wait_ge(*count.last)
                    tt(dst[:, 0], dst[:, 0], sc[1][:, 1, :, 0:n], ALU.subtract).then_inc(count.up(dve_steps), 1)
                    tt(dst[:, 1], dst[:, 1], sc[1][:, 0, :, 0:n], ALU.add).then_inc(count.up(scanned), 1)
                elif k == "sfinal":
                    vector.wait_ge(*count.last)
                    src = Hb[:, :, :, NPC - 1:NCH]
                    for q in range(2):
                        c = sq8[:, q, 0, :].unsqueeze(1).unsqueeze(3).to_broadcast([P, 2, GP, 9])
                        tt(t9[q][:], src, c, ALU.mult).then_inc(count.up(dve_steps), 1)
                    vector.wait_ge(*count.last)
                    tt(Fh[:], Fh[:], t9[0][:], ALU.add).then_inc(count.up(dve_steps), 1)
                    vector.wait_ge(*count.last)
                    tt(Fh[:, 0], Fh[:, 0], t9[1][:, 1], ALU.subtract).then_inc(count.up(dve_steps), 1)
                    tt(Fh[:, 1], Fh[:, 1], t9[1][:, 0], ALU.add).then_inc(count.up(dve_steps), 1)
                    vector.wait_ge(*count.last)
                    nc.vector.tensor_copy(Fo[:].rearrange("q i (n p) -> q i p n", p=GP), Fh[:]).then_inc(count.up(fo_ready), 1)
                elif k == "pairqk":
                    p = a[0]
                    vector.wait_ge(qk_hi, 2 * p + 2)
                    lower(klo[:], qk[:, 1, p, 0:TP], khi[:]).then_inc(count.up(qk_lo), 1)
                    lower(qlo[:], qk[:, 0, p, 0:TP], qhi[:]).then_inc(count.up(qk_lo), 1)
                elif k == "pairv":
                    p = a[0]
                    vector.wait_ge(v_hi, p + 1)
                    vv = [x[:].rearrange("s (b c) -> s b c", b=4) for x in (vlo, vhi)]
                    lower(vv[0], vtok[:, 0:4, P * p:P * p + P], vv[1]).then_inc(count.up(v_lo), 1)
                elif k in ("z", "sl"):
                    h = a[0] if k == "z" else H
                    ta_, tb = t1[h % 2], t2[h % 2]
                    vector.wait_ge(*((z_ready, h + 1) if h < H else (kt_used, SB * NPG)))
                    if h >= 2:
                        vector.wait_ge(w_ready, h - 1)
                    for rows, c0, c1 in piece_list(h):
                        b = bias[0:rows, h:h + 1] if h < H else 0.0
                        nc.vector.tensor_scalar(tb[0:rows, c0:c1], zflat(h, rows, c0, c1), b, None,
                                                ALU.add).then_inc(count.up(dve_steps), 1)
                    vector.wait_ge(*count.last)
                    for rows, c0, c1 in piece_list(h):
                        z = tb[0:rows, c0:c1]
                        nc.vector.scalar_tensor_tensor(out=ta_[0:rows, c0:c1], in0=z, scalar=-1.0, in1=z,
                                                       op0=ALU.mult, op1=ALU.min).then_inc(
                            count.up(z_abs if c1 > 1024 else dve_steps), 1)
                    vector.wait_ge(l_ready, h + 1)
                    for rows, c0, c1 in piece_list(h):
                        nc.vector.scalar_tensor_tensor(out=tb[0:rows, c0:c1], in0=tb[0:rows, c0:c1], scalar=0.0,
                                                       in1=ta_[0:rows, c0:c1], op0=ALU.max, op1=ALU.add).then_inc(
                            count.up(L_raw if c1 > 1024 else dve_steps), 1)
                elif k == "lsplit":
                    h = a[0]
                    hi, lo = Lsp[h % 2]
                    vector.wait_ge(L_hi, h + 1)
                    for rows, c0, c1 in piece_list(h):
                        lower(lo[0:rows, c0:c1], t2[h % 2][0:rows, c0:c1], hi[0:rows, c0:c1]).then_inc(
                            count.up(L_ready if c1 > 1024 else dve_steps), 1)
                elif k == "wsplit":
                    h = a[0]
                    hi, lo = Lsp[h % 2]
                    vector.wait_ge(W_hi, h + 1)
                    lower(lo[:, 0:ZW], t1[h % 2][:, 0:ZW], hi[:, 0:ZW]).then_inc(count.up(w_ready), 1)
                elif k == "av":
                    h = a[0]
                    r = 64 * (h % 2)
                    if h == 0:
                        vector.wait_ge(stored, 16 * 7)
                    vector.wait_ge(o_hi, count.next(o_hi))
                    lower(oT[1][r:r + 64, h // 2, 0:TP], bank(e)[r:r + 64, :], oT[0][r:r + 64, h // 2, 0:TP]).then_inc(
                        count.upto(*read(e)), 1)
                elif k == "sz":
                    vector.wait_ge(brow_in, 16)
                    nc.vector.tensor_copy(brow[:].rearrange("o (b h t) -> o b h t", b=SB, h=H),
                                         sbr[:].unsqueeze(1).unsqueeze(3).to_broadcast([1, SB, H, ST])).then_inc(count.up(dve_steps), 1)
                    nc.vector.memset(Qb[:], 0.0).then_inc(count.up(dve_steps), 1)
                    vector.wait_ge(*count.last)
                    for h2 in range(2):
                        nc.vector.tensor_copy(Qb[64 * h2:64 * h2 + 64, :, :, 8 * h2:8 * h2 + 8],
                                             qk[64 * h2:64 * h2 + 64, 0, :, TP:T].rearrange("q p (b t) -> q b p t", t=ST)).then_inc(count.up(qb_ready), 1)
                elif k == "sav":
                    for h2 in range(2):
                        vector.wait_ge(o_hi, count.next(o_hi))
                        lower(sample_cols(oT[1], h2), sample_out(h2), sample_cols(oT[0], h2)).then_inc(
                            count.upto(*read("sav")) if h2 else count.up(dve_steps), 1)
                elif k == "ysplit":
                    vector.wait_ge(y_hi, count.next(y_hi))
                    lower(yh[1][:], yact[:], yh[0][:]).then_inc(count.up(y_lo), 1)
                elif k == "msinv":
                    w = a[0]
                    if w == 0:
                        for half, ab in enumerate("ab"):
                            vector.wait_ge(*full(("ms", 0, ab)))
                            nc.vector.tensor_scalar(inv[:, HT * half:HT * half + HT], banks[:, half, 0:HT], 1.0 / D, EPS,
                                                       ALU.mult, ALU.add).then_inc(count.upto(*read(("ms", 0, ab))), 1)
                        vector.wait_ge(*count.last)
                    else:
                        vector.wait_ge(*read(("ms", 1, "a")))
                        vector.wait_ge(*read(("ms", 1, "b")))
                    nc.vector.reciprocal(inv[:], inv[:]).then_inc(count.up(dve_steps), 1)
                    vector.wait_ge(*count.last)
                elif k == "pT":
                    t = a[0]
                    t0, n = TOK[t]
                    vector.wait_ge(pT_hi, count.next(pT_hi))
                    lower(pT[1][:, :, t0:t0 + n], bank(e)[:, 0:2 * P].rearrange("p (k n) -> p k n", k=2)[:, :, 0:n],
                          pT[0][:, :, t0:t0 + n]).then_inc(count.upto(*read(e)), 1)

        @block.tensor
        def _(tensor):
            count = Count()

            def mm(out, lhsT, rhs, start=False, stop=False):
                return nc.tensor.matmul(out, lhsT, rhs, start=start, stop=stop, skip_group_check=True)

            def three(out, w, x, start=False, stop=False):
                mm(out, w[0], x[0], start=start)
                mm(out, w[0], x[1])
                return mm(out, w[1], x[0], stop=stop)

            def operand(u):
                kind, m0, nk, nm = units[u]
                if kind in ("attn",):
                    return oT
                if kind in ("val", "glu"):
                    return yh
                if kind == "out":
                    return mg
                if kind == "down":
                    return hid[m0 // 8 % 2]
                if kind == "ple":
                    return pT
                return act

            def unit(u):
                kind, m0, nk, nm = units[u]
                tensor.wait_ge(w_lo, u + 1)
                x = operand(u)
                if u == 0:
                    tensor.wait_ge(h_lo, 10)
                if u == FIRST["attn"]:
                    tensor.wait_ge(*read("sav"))
                if u == FIRST["val"]:
                    tensor.wait_ge(y_lo, 1)
                if u == FIRST["ple"]:
                    tensor.wait_ge(*read(("pT", 4)))
                wh, wl = [wview(w, u % NSPLIT, u) for w in (whi, wlo)]
                for j in range(nm):
                    job = ("m", u, j)
                    if used_before(job):
                        tensor.wait_ge(*free(job))
                    out = dplace(job)
                    c = slice(P * j, P * j + P)
                    for k in range(nk):
                        if u == FIRST["out"]:
                            tensor.wait_ge(mg_lo, k + 1)
                        if u == FIRST["up"]:
                            tensor.wait_ge(act_lo, k + 1)
                        if u == FIRST["pgate"]:
                            tensor.wait_ge(act_lo, KT + k + 1)
                        if kind == "down" and j == 0 and m0 % 8 == 0:
                            tensor.wait_ge(hid_lo, 4 * (m0 // 8) + k + 1)
                        for w, xx, first, last in ((wh, x[0], k == 0, False), (wh, x[1], False, False),
                                                   (wl, x[0], False, k == nk - 1)):
                            for half in range(2):
                                ins = mm(out[:, half, 0:HT], w[:, k, c], xx[:, k, HT * half:HT * half + HT],
                                         start=first, stop=last)
                    ins.then_inc(full_of(job), 1)

            def transpose(out, in_, rows=P):
                return nc.tensor.transpose(out, in_, ident[0:rows, 0:rows])

            def page_scores(j):
                b, page = j // NPG, j % NPG
                tensor.wait_ge(*read(("skt", j)))
                for p in range(AT):
                    c = 16 * (AT * b + p)
                    ins = mm(banks[:, page, c:c + 16], KTb[:, j % 2, P * p:P * p + P], Qb[:, b, p, :], stop=True)
                ins.then_inc(kt_used, 1)

            for e in schedule:
                k, a = e[0], e[1:]
                if k == "h":
                    t, half = a
                    n = TOK[t][1]
                    if t == 0 and half == 0:
                        tensor.wait_ge(ident_ready, 1)
                    tensor.wait_ge(xn_ready, t + 1)
                    if used_before(e):
                        tensor.wait_ge(*free(e))
                    for c in range(4):
                        c0 = P * (4 * half + c)
                        ins = transpose(bank(e)[:, P * c:P * c + n], xtok[0:n, t, c0:c0 + P], n)
                    ins.then_inc(full_of(e), 1)
                elif k == "s5ct":
                    tensor.wait_ge(params_in, 16 * N_PARAMS)
                    if used_before(e[0]):
                        tensor.wait_ge(*free(e[0]))
                    for c in range(4):
                        ins = transpose(bank("s5ct")[:, P * c:P * c + P], cnat[:, c // 2, c % 2, :])
                    ins.then_inc(full_of("s5ct"), 1)
                elif k == "s5h0":
                    if used_before("s5h0"):
                        tensor.wait_ge(*free("s5h0"))
                    for c in range(2):
                        ins = transpose(bank("s5h0")[:, P * c:P * c + P], snat[:, c:2 * P:2])
                    ins.then_inc(full_of("s5h0"), 1)
                elif k == "unit":
                    unit(a[0])
                elif k == "qksum":
                    p = a[0]
                    if p == 0:
                        tensor.wait_ge(consts_ready, 1)
                        if used_before("qs0"):
                            tensor.wait_ge(*free("qs0"))
                        if used_before("qs1"):
                            tensor.wait_ge(*free("qs1"))
                    tensor.wait_ge(sq_ready, p + 1)
                    for half in range(2):
                        ins = mm(banks[0:16, half, 0:HT], hsum[:, p, :], gst[:, p % 2, HT * half:HT * half + HT],
                                 start=p == 0, stop=p == 7)
                        if p == 7 and half == 0:
                            ins.then_inc(full_of("qs0"), 1)
                    if p == 7:
                        ins.then_inc(full_of("qs1"), 1)
                    else:
                        ins.then_inc(sq_used, 1)
                elif k == "qknorm":
                    p, half = a
                    if p == 0 and half == 0:
                        tensor.wait_ge(nrm_ready, 1)
                    if used_before(e):
                        tensor.wait_ge(*free(e))
                    mm(bank(e)[:, 0:HT], sel[:, p, :], nrm[:, HT * half:HT * half + HT], True, True).then_inc(full_of(e), 1)
                elif k == "gt":
                    part, n = a
                    tensor.wait_ge(gnat_ready, part + 1)
                    if used_before(e):
                        tensor.wait_ge(*free(e))
                    for c in range(4):
                        ins = transpose(bank(e)[:, P * c:P * c + P],
                                        gnat[:, 4 * n + c].rearrange("q j c -> q (j c)"))
                    ins.then_inc(full_of(e), 1)
                elif k == "vs":
                    tensor.wait_ge(ca_ready, 1)
                    if used_before(e):
                        tensor.wait_ge(*free(e))
                    for c in range(4):
                        g = 8 * (a[0] // 2) + a[0] % 2 + 2 * c
                        r = slice(64 * (g % 2), 64 * (g % 2) + 64)
                        out = bank(e)[0:GC, P * c:P * c + P]
                        for part in range(2):
                            ins = mm(out, bb[r, part, g // 2, :], CA[r, part, g // 2, 0:CH, :].rearrange("q k c -> q (k c)"),
                                     part == 0, part == 1)
                    ins.then_inc(full_of(e), 1)
                elif k in ("kout", "vout"):
                    t = a[0]
                    t0, n = TOK[t]
                    if t == 0:
                        tensor.wait_ge(*read(("qknorm", 7, 1) if k == "kout" else ("m", FIRST["v"] + 3, 0)))
                        tensor.wait_ge(*read(("qknorm", 7, 0) if k == "kout" else ("m", FIRST["v"] + 2, 0)))
                    if used_before(e):
                        tensor.wait_ge(*free(e))
                    for p in range(AT):
                        src = qk[:, 1, p, t0:t0 + n] if k == "kout" else vT[:, p, t0:t0 + n]
                        ins = transpose(bank(e)[0:n, P * p:P * p + P], src)
                    ins.then_inc(full_of(e), 1)
                elif k == "ut":
                    q, half = a
                    tensor.wait_ge(*read(("m", FIRST["u"] + q, 0)))
                    if used_before(e):
                        tensor.wait_ge(*free(e))
                    for c in range(4):
                        j = 4 * half + c
                        ins = transpose(bank(e)[0:NCH, P * c:P * c + P], uT[:, q, j:T:CH])
                    ins.then_inc(full_of(e), 1)
                elif k == "ug":
                    q, half = a
                    for hh in range(2):
                        tensor.wait_ge(*read(("ut", q, hh)))
                    if used_before(e):
                        tensor.wait_ge(*free(e))
                    for c in range(4):
                        src = up_[0:NCH, q % 2, 4 * half + c].rearrange("n j c -> n (j c)")
                        ins = transpose(bank(e)[:, NCH * c:NCH * c + NCH], src, NCH)
                    ins.then_inc(full_of(e), 1)
                elif k == "s":
                    n, part = a
                    if n == 0:
                        for hh in range(2):
                            tensor.wait_ge(*read(("ug", 3, hh)))
                            tensor.wait_ge(*read(("gt", part, 2 + hh)))
                    if used_before(e):
                        tensor.wait_ge(*free(e))
                    for c in range(4):
                        p = 4 * n + c
                        for g2 in range(2):
                            r = slice(64 * g2, 64 * g2 + 64)
                            ins = mm(bank(e)[r, NCH * c:NCH * c + NCH], GT[:, part, p, r], UT[:, 2 * p + g2, :], True, True)
                    ins.then_inc(full_of(e), 1)
                elif k == "sfinal":
                    tensor.wait_ge(fo_ready, 1)
                    if used_before(k):
                        tensor.wait_ge(*free(k))
                    for part in range(2):
                        transpose(banks[:, 0, P * part:P * part + P], Fo[:, part, GP:9 * GP])
                    for part in range(2):
                        ins = transpose(banks[0:GP, 0, P * (2 + part):P * (3 + part)], Fo[:, part, 0:GP])
                    ins.then_inc(full_of(k), 1)
                elif k == "y":
                    q, half = a
                    if q == 0 and half == 0:
                        tensor.wait_ge(t_in, 16 * CH)
                        tensor.wait_ge(scanned, 6)
                    if used_before(e):
                        tensor.wait_ge(*free(e))
                    for c in range(4):
                        g = 8 * q + 2 * c + half
                        r = slice(64 * (g % 2), 64 * (g % 2) + 64)
                        out = bank(e)[0:NCH, P * c:P * c + P]
                        mm(out, UT[:, g, :], Tm[:, g, :], True)
                        for part in range(2):
                            ins = mm(out, Hb[r, part, g // 2, :],
                                     CA[r, part, g // 2, 1:CH + 1, :].rearrange("q k c -> q (k c)"), False, part == 1)
                    ins.then_inc(full_of(e), 1)
                elif k == "yt":
                    q, half = a
                    for hh in range(2):
                        tensor.wait_ge(*read(("y", q, hh)))
                    if used_before(e):
                        tensor.wait_ge(*free(e))
                    for c in range(4):
                        ins = transpose(bank(e)[:, NCH * c:NCH * c + NCH], yb[0:NCH, q % 2, 4 * half + c, :], NCH)
                    ins.then_inc(full_of(e), 1)
                elif k == "z":
                    h = a[0]
                    r = slice(64 * (h % 2), 64 * (h % 2) + 64)
                    if h < 2:
                        for n in ((0, 1, 2), (4, 5))[h]:
                            tensor.wait_ge(psum_free[n], jobs["z_before"][n])
                    else:
                        tensor.wait_ge(z_free, h - 1)
                    tensor.wait_ge(qk_lo, 2 * (h // 2) + 2)
                    for b in (0, 1, 3, 2):
                        w = TP - P * b
                        out = zflat(h, P, ZOFF[b], ZOFF[b] + w)
                        ins = three(out, [x[r, P * b:P * b + P] for x in (khi, klo)],
                                    [x[r, P * b:TP] for x in (qhi, qlo)], start=b != 3)
                    ins.then_inc(z_ready, 1)
                elif k == "cum":
                    h = a[0]
                    tensor.wait_ge(L_ready, h + 1)
                    for b in range(4):
                        for c in range(b, 4):
                            w = TP - P * c
                            o0 = ZOFF[b] + P * (c - b)
                            for L in Lsp[h % 2]:
                                ins = mm(zflat(h, P, o0, o0 + w), (tri if c == b else negs)[:, :], L[:, ZOFF[c]:ZOFF[c] + w],
                                         stop=True)
                    ins.then_inc(cum_ready, 1)
                elif k == "av":
                    h = a[0]
                    tensor.wait_ge(w_ready, h + 1)
                    tensor.wait_ge(v_lo, h // 2 + 1)
                    if used_before(e):
                        tensor.wait_ge(*free(e))
                    for b in range(4):
                        ins = three(bank(e)[:, P * b:TP], [x[:, P * b:P * b + P] for x in (vhi, vlo)],
                                    [x[:, ZOFF[b]:ZOFF[b] + TP - P * b] for x in Lsp[h % 2]], start=b == 0, stop=b == 3)
                    ins.then_inc(full_of(e), 1)
                elif k == "sz":
                    tensor.wait_ge(z_free, H)
                    tensor.wait_ge(*read(("av", H - 1)))
                    tensor.wait_ge(qb_ready, 2)
                    for n in range(3):
                        rows = P if n < 2 else ST
                        mm(banks[0:rows, n, :], ones[0:1, 0:rows], brow[:], True)
                    for b in range(SB):
                        for p in range(AT):
                            c = 16 * (AT * b + p)
                            mm(banks[0:ST, 2, c:c + 16], qk[:, 1, p, TP + ST * b:TP + ST * b + ST], Qb[:, b, p, :], stop=True)
                elif k == "skt":
                    j = a[0]
                    tensor.wait_ge(page_in[j % NPAGE], 16 * (j // NPAGE + 1))
                    if used_before(e):
                        tensor.wait_ge(*free(e))
                    for p in range(AT):
                        ins = transpose(dplace(e)[:, 0, P * p:P * p + P], pages[:, j % NPAGE, P * p:P * p + P])
                    ins.then_inc(full_of(e), 1)
                    if j:
                        page_scores(j - 1)
                elif k == "sl":
                    page_scores(SB * NPG - 1)
                elif k == "scum":
                    tensor.wait_ge(L_ready, H + 1)
                    new = slice(1024, SZW)
                    for L in Lsp[0]:
                        mm(banks[0:ST, 2, :], tri[0:ST, 0:ST], L[0:ST, new], stop=True)
                        mm(banks[:, 1, :], tri[:, :], L[:, 512:1024])
                        mm(banks[:, 1, :], negs[0:ST, :], L[0:ST, new], stop=True)
                        mm(banks[:, 0, :], tri[:, :], L[:, 0:512])
                        mm(banks[:, 0, :], negs[:, :], L[:, 512:1024])
                        ins = mm(banks[:, 0, :], negs[0:ST, :], L[0:ST, new], stop=True)
                    ins.then_inc(cum_ready, 1)
                elif k == "sav":
                    tensor.wait_ge(w_masked, 4 * H + 1)
                    tensor.wait_ge(z_free, H + 1)
                    if used_before(k):
                        tensor.wait_ge(*free(k))
                    for b in range(SB):
                        for page in range(NPG):
                            n = SB * NPG + NPG * b + page
                            tensor.wait_ge(page_in[n % NPAGE], 16 * (n // NPAGE + 1))
                        tensor.wait_ge(vnew_in[b % NVNEW], 16 * (b // NVNEW + 1))
                        for p in range(AT):
                            c = 16 * (AT * b + p)
                            out = bank(k)[:, c:c + 16]
                            vc = slice(P * p, P * p + P)
                            for page in range(NPG):
                                mm(out, pages[:, (SB * NPG + NPG * b + page) % NPAGE, vc],
                                   t1[0][:, 512 * page + c:512 * page + c + 16], page == 0)
                            ins = mm(out, vnew[:, b % NVNEW, vc], t1[0][0:ST, 1024 + c:1024 + c + 16], stop=True)
                        if b < SB - 1:
                            ins.then_inc(vb_used, 1)
                        else:
                            ins.then_inc(full_of(k), 1)
                elif k == "xT":
                    t, half = a
                    n = TOK[t][1]
                    tensor.wait_ge(x2_in[t % 2], 16 * (t // 2 + 1))
                    if used_before(e):
                        tensor.wait_ge(*free(e))
                    for c in range(4):
                        c0 = P * (4 * half + c)
                        ins = transpose(dplace(e)[:, 0, P * c:P * c + n], xtok2[0:n, t % 2, c0:c0 + P], n)
                    ins.then_inc(full_of(e), 1)
                elif k == "ms":
                    w, m = a
                    if m == 0:
                        if used_before(("ms", w, "a")):
                            tensor.wait_ge(*free(("ms", w, "a")))
                        if used_before(("ms", w, "b")):
                            tensor.wait_ge(*free(("ms", w, "b")))
                        if w == 0:
                            tensor.wait_ge(z_free, H + 1)
                    tensor.wait_ge(ms_sq, KT * w + m + 1)
                    for half, ab in enumerate("ab"):
                        ins = mm(banks[:, half, 0:HT], ones[:, :], sq[:, m % 2, HT * half:HT * half + HT], m == 0, m == KT - 1)
                        if m == KT - 1:
                            ins.then_inc(full_of(("ms", w, ab)), 1)
                    if m < KT - 1:
                        ins.then_inc(ms_used, 1)
                elif k == "pT":
                    t = a[0]
                    t0, n = TOK[t]
                    tensor.wait_ge(p_in[t % 2], 16 * (t // 2 + 1))
                    if used_before(e):
                        tensor.wait_ge(*free(e))
                    for c in range(2):
                        ins = transpose(bank(e)[:, P * c:P * c + n], ptok[0:n, t % 2, P * c:P * c + P], n)
                    ins.then_inc(full_of(e), 1)
                elif k == "yout":
                    m = a[0]
                    tensor.wait_ge(yf_ready, m + 1)
                    if used_before(("yout", m, "a")):
                        tensor.wait_ge(*free(("yout", m, "a")))
                    for t in range(4):
                        ins = transpose(banks[:, 2, P * t:P * t + P], yf[:, m % 2, P * t:P * t + P])
                    ins.then_inc(full_of(("yout", m, "a")), 1)
                    if used_before(("yout", m, "b")):
                        tensor.wait_ge(*free(("yout", m, "b")))
                    transpose(banks[0:TS, 3, 0:P], yf[:, m % 2, TP:T]).then_inc(full_of(("yout", m, "b")), 1)


INS = ["x_prompt", "x_sample", "p_prompt", "p_sample", "cache_k", "cache_v", "state_ssm", "page_table",
       "g_mix", "w_in", "g_q", "g_k", "sb_bias", "w_attn_out", "ssm_a_re", "ssm_a_im", "ssm_log_dt",
       "ssm_b_re", "ssm_b_im", "ssm_c_re", "ssm_c_im", "ssm_d", "w_glu_val", "w_glu_gate", "w_out",
       "g_mlp", "w_up", "w_down", "g_ple", "w_ple", "w_ple_gate"]
OUTS = [("y_prompt", (1, TP, D)), ("y_sample", (SB, ST, D)), ("k_prompt", (1, 1, TP, H, HD)),
        ("v_prompt", (1, 1, TP, H, HD)), ("ssm_prompt", (1, 1, G, NS, 2)), ("k_sample", (1, SB, ST, H, HD)),
        ("v_sample", (1, SB, ST, H, HD)), ("ssm_sample", (1, SB, G, NS, 2))]


def kernel(**inputs):
    import concourse.bacc as bacc
    from concourse.bass_utils import run_bass_kernel_spmd as run

    nc = bacc.Bacc("TRN2", target_bir_lowering=False, num_devices=1)
    arrays, i, o = {}, {}, {}
    for name in INS:
        a = np.ascontiguousarray(inputs[name])
        arrays[f"in_{name}"] = a
        i[name] = nc.dram_tensor(f"in_{name}", a.shape, mybir.dt.from_np(a.dtype), kind="ExternalInput").ap()
    for name, shape in OUTS:
        o[name] = nc.dram_tensor(f"out_{name}", shape, F32, kind="ExternalOutput").ap()
    build(nc, i, o)
    r = run(nc, [arrays], core_ids=[0])
    return tuple(r.results[0][f"out_{name}"] for name, _ in OUTS)
```

```python
from contextlib import ExitStack

import numpy as np

import concourse.bass as bass
from concourse import mybir

ALU = mybir.AluOpType
ACT = mybir.ActivationFunctionType
F32 = mybir.dt.float32
F32R = mybir.dt.float32r
I32 = mybir.dt.int32

P = 128
D = 1024
KT = D // P
TP = 512
SB, ST = 8, 8
TS = SB * ST
T = TP + TS
HT = T // 2
H, HD = 8, 64
AW = H * HD
AT = AW // P
NPG = 2
PLE = 256
G, GC, NS = 32, 16, 64
GP = G // 2
CH = 8
NCH = T // CH
NPC = TP // CH
EPS = 1e-6
NPAGE = 10
UW = 1024
NRAW, NSPLIT = 5, 3
TOK = [(128 * i, 128) for i in range(4)] + [(TP, TS)]
PI = float(np.pi)
C1 = 6.28125
C2 = float(np.float32(2 * np.pi - C1))
C3 = float(2 * np.pi - C1 - C2)
MAGIC = 12582912.0
ZOFF = {0: 0, 1: 512, 3: 896, 2: 1024}
ZW = 1280
SZW = 3 * 512


def units_of():
    us = [("q", i, 8, 1) for i in range(AT)] + [("k", i, 8, 1) for i in range(AT)]
    us += [("u", i, 8, 1) for i in range(AT)]
    us += [("gate", i, 8, 1) for i in range(9)]
    us += [("v", i, 8, 1) for i in range(AT)]
    us += [("gate", i, 8, 1) for i in range(9, 16)]
    for i in range(4):
        us += [("attn", 2 * i, 4, 2), ("val", 2 * i, 4, 2), ("glu", 2 * i, 4, 2)]
    us += [("out", i, 8, 1) for i in range(KT)]
    us += [("up", i, 8, 1) for i in range(4)]
    for f in range(8):
        for i in range(4):
            if f < 7:
                us.append(("up", 4 * (f + 1) + i, 8, 1))
            us.append(("down", 8 * f + 2 * i, 4, 2))
    us += [("ple", 0, 2, 4), ("ple", 4, 2, 4)]
    us += [("pgate", i, 8, 1) for i in range(KT)]
    return us


DENSE = 4
LASTBANK = 6


def schedule_of(units):
    ev, jobs, uses = [], {}, [0] * 7
    n, dense = [0], [0]

    def job(name, place):
        jobs[name] = (place, uses[place])
        uses[place] += 1

    def dense_job(name):
        job(name, DENSE + dense[0] % 2)
        dense[0] += 1

    def event(*name, place=None):
        ev.append(name)
        if place is not None:
            job(name if len(name) > 1 else name[0], place)

    def unit(k=1):
        for _ in range(k):
            event("unit", n[0])
            for j in range(units[n[0]][3]):
                dense_job(("m", n[0], j))
            n[0] += 1

    event("norm", 0)
    for t in range(5):
        if t < 4:
            event("norm", t + 1)
        for half in range(2):
            event("h", t, half, place=(2 * t + half) % 4)
        event("hlo", t)
        if t == 3:
            event("split0", 0)
    event("split0", 1)
    event("split0", 2)
    event("s5small")
    event("s5ct", place=2)
    event("s5h0", place=3)
    event("s5big", 0)
    job("qs0", 0)
    job("qs1", 1)
    for p in range(8):
        unit()
        if p:
            event("qksum", p - 1)
    unit()
    event("qksum", 7)
    event("qkrstd")
    unit()
    for i in range(4):
        event("gt", 0, i, place=2 + i % 2)
    event("s5big", 1)
    for p in range(8):
        for half in range(2):
            event("qknorm", p, half, place=half)
        if p in (1, 4):
            unit()
    for i in range(4):
        event("gt", 1, i, place=2 + i % 2)
    for q in range(4):
        event("kout", q, place=q % 2)
        for half in range(2):
            event("ut", q, half, place=half)
        for half in range(2):
            event("ug", q, half, place=2 + half)
    event("kout", 4, place=0)
    for i in range(4):
        for part in range(2):
            event("s", i, part, place=2 * (i % 2) + part)
    event("tzero")
    for lvl in range(6):
        event("scan", lvl)
        unit()
        if lvl < 4:
            for i in (2 * lvl, 2 * lvl + 1):
                event("vs", i, place=2 + i % 2)
        if lvl == 3:
            event("vd")
            event("tload")
        if lvl >= 3:
            unit()
    for q in range(4):
        for half in range(2):
            event("y", q, half, place=half)
        for half in range(2):
            event("yt", q, half, place=2 + half)
        if q % 2 == 0:
            unit()
    event("pairqk", 0)
    event("sfinal", place=0)
    jobs["z_before", 0] = list(enumerate(uses[:3]))
    event("z", 0)
    unit()
    event("zln", 0)
    unit()
    event("lsplit", 0)
    for t in range(5):
        event("vout", t)
        dense_job(("vout", t))
    jobs["z_before", 1] = [(place, uses[place]) for place in (4, 5)]
    event("z", 1)
    event("pairqk", 1)
    event("zln", 1)
    for h in range(H):
        event("cum", h)
        if h:
            event("av", h - 1, place=3 if h % 2 else LASTBANK)
        if h == H - 1:
            event("sz")
        if h < H - 1:
            event("lsplit", h + 1)
        if h + 2 < H:
            event("z", h + 2)
            if h % 2 and h + 3 < H:
                event("pairqk", (h + 3) // 2)
        event("wsplit", h)
        if h:
            event("oout", h - 1)
        if h % 2 == 0:
            event("pairv", h // 2)
        if h + 2 < H:
            event("zln", h + 2)
        if h:
            event("olow", h - 1)
    event("av", H - 1, place=LASTBANK)
    event("oout", H - 1)
    event("olow", H - 1)
    unit()
    for j in range(SB * NPG):
        event("skt", j)
        dense_job(("skt", j))
        if j == 5:
            unit()
    event("sl")
    event("zln", H)
    unit()
    event("lsplit", H)
    unit()
    event("scum")
    event("ysplit")
    job("sav", 3)
    unit()
    for quarter in range(4):
        event("sav", quarter)
        if quarter == 1:
            unit()
    event("merge")
    unit()
    for i in range(4):
        for j in range(3):
            unit()
            for t in ((0, 1), (2, 3), (4,))[j] if i == 3 else ():
                for half in range(2):
                    event("xT", t, half)
                    dense_job(("xT", t, half))
    for m in range(KT):
        unit()
        if m:
            event("ms", 0, m - 1)
    job(("ms", 0, "a"), 0)
    job(("ms", 0, "b"), 1)
    unit()
    event("ms", 0, KT - 1)
    event("msinv", 0)
    unit(3)
    for f in range(7):
        unit(8)
    job(("ms", 1, "a"), 0)
    job(("ms", 1, "b"), 1)
    for i in range(4):
        for t in ((0, 1), (2, 3), (4,), ())[i]:
            event("pT", t, place=2 + t % 2)
        unit()
        if i:
            event("ms", 1, 2 * i - 2)
            event("ms", 1, 2 * i - 1)
    unit(2)
    event("ms", 1, 6)
    event("ms", 1, 7)
    event("msinv", 1)
    for m in range(KT + 1):
        if m < KT:
            unit()
        if m:
            event("yout", m - 1)
            job(("yout", m - 1, "a"), 2)
            job(("yout", m - 1, "b"), 3)
    assert n[0] == len(units), (n[0], len(units))
    return ev, jobs


class Count:

    def __init__(self):
        self.made, self.waited, self.last = {}, {}, None

    def up(self, sem):
        self.made[sem] = self.made.get(sem, 0) + 1
        self.last = (sem, self.made[sem])
        return sem

    def upto(self, sem, count):
        self.last = (sem, count)
        return sem

    def next(self, sem):
        self.waited[sem] = self.waited.get(sem, 0) + 1
        return self.waited[sem]


def build(nc, i, o):
    units = units_of()
    schedule, jobs = schedule_of(units)
    ctx = ExitStack()
    with ctx:
        def semaphore(name):
            return ctx.enter_context(nc.semaphore(name))

        def ring(name, slots):
            return [semaphore(f"{name}{slot}") for slot in range(slots)]

        ident_ready = semaphore("ident_ready")
        consts_ready = semaphore("consts_ready")
        gmix_in = semaphore("gmix_in")
        params_in = semaphore("params_in")
        sd_ready = semaphore("sd_ready")
        xn_ready = semaphore("xn_ready")
        h_hi = semaphore("h_hi")
        h_lo = semaphore("h_lo")
        w_hi = semaphore("w_hi")
        w_lo = semaphore("w_lo")
        act_hi = semaphore("act_hi")
        act_lo = semaphore("act_lo")
        sq_ready = semaphore("sq_ready")
        sq_used = semaphore("sq_used")
        nrm_ready = semaphore("nrm_ready")
        dt_ready = semaphore("dt_ready")
        theta_ready = semaphore("theta_ready")
        trig_ready = semaphore("trig_ready")
        s5_powers = semaphore("s5_powers")
        s5_bb = semaphore("s5_bb")
        ca_ready = semaphore("ca_ready")
        gnat_ready = semaphore("gnat_ready")
        vs_ready = semaphore("vs_ready")
        tm_zero = semaphore("tm_zero")
        vs_spilled = semaphore("vs_spilled")
        t_in = semaphore("t_in")
        scanned = semaphore("scanned")
        fo_ready = semaphore("fo_ready")
        qk_hi = semaphore("qk_hi")
        qk_lo = semaphore("qk_lo")
        v_hi = semaphore("v_hi")
        v_lo = semaphore("v_lo")
        z_ready = semaphore("z_ready")
        z_copied = semaphore("z_copied")
        z_abs = semaphore("z_abs")
        l_ready = semaphore("l_ready")
        L_raw = semaphore("L_raw")
        L_masked = semaphore("L_masked")
        L_hi = semaphore("L_hi")
        L_ready = semaphore("L_ready")
        cum_ready = semaphore("cum_ready")
        z_free = semaphore("z_free")
        w_masked = semaphore("w_masked")
        W_hi = semaphore("W_hi")
        w_ready = semaphore("w_ready")
        o_hi = semaphore("o_hi")
        table_in = semaphore("table_in")
        brow_in = semaphore("brow_in")
        qb_ready = semaphore("qb_ready")
        kt_used = semaphore("kt_used")
        vb_used = semaphore("vb_used")
        y_hi = semaphore("y_hi")
        y_lo = semaphore("y_lo")
        gl_sig = semaphore("gl_sig")
        mg_ready = semaphore("mg_ready")
        mg_hi = semaphore("mg_hi")
        mg_lo = semaphore("mg_lo")
        mg_done = semaphore("mg_done")
        xf_ready = semaphore("xf_ready")
        ms_sq = semaphore("ms_sq")
        ms_used = semaphore("ms_used")
        hs_ready = semaphore("hs_ready")
        hid_hi = semaphore("hid_hi")
        hid_lo = semaphore("hid_lo")
        pT_hi = semaphore("pT_hi")
        ysg_ready = semaphore("ysg_ready")
        yf_ready = semaphore("yf_ready")
        stored = semaphore("stored")
        y_stored = semaphore("y_stored")
        act_steps = semaphore("act_steps")
        dve_steps = semaphore("dve_steps")
        pool_steps = semaphore("pool_steps")
        raw_in = ring("raw_in", NRAW)
        x_in = ring("x_in", 5)
        x2_in = ring("x2_in", 2)
        p_in = ring("p_in", 2)
        page_in = ring("page_in", NPAGE)
        vnew_in = ring("vnew_in", SB)
        gl_in = ring("gl_in", 2)
        gate_out = ring("gate_out", 2)
        k_stored = ring("k_stored", 2)
        psum_full = ring("psum_full", 7)
        psum_free = ring("psum_free", 7)

        def sb(name, shape, dt=F32):
            return ctx.enter_context(nc.sbuf_tensor(name, shape, dt))

        wraw = sb("wraw", [P, NRAW, UW])
        whi = sb("whi", [P, NSPLIT, UW], F32R)
        wlo = sb("wlo", [P, NSPLIT, UW], F32R)
        act = [sb(f"act_{n}", [P, KT, T], F32R) for n in ("hi", "lo")]
        ident = sb("ident", [P, P])
        ones = sb("ones", [P, P])
        tri = sb("tri", [P, P], F32R)
        negs = sb("negs", [P, P], F32R)
        gains = sb("gains", [P, 3, KT])
        gqk = sb("gqk", [P, 2])
        bias = sb("bias", [P, H])
        stat = sb("stat", [P, 3, 5])
        eps = sb("eps", [P, 1])
        halfpi = sb("halfpi", [P, 1])
        hsum = sb("hsum", [P, 8, 16])

        def placed(offset, name, shape, dt=F32):
            with ExitStack() as s:
                if offset:
                    s.enter_context(nc.sbuf_tensor(f"below_{name}", [P, offset // 4], F32))
                return s.enter_context(nc.sbuf_tensor(name, shape, dt))

        yact = placed(0, "yact", [P, AT, T])
        oT = [placed(9216 * (1 + n), f"oT{n}", [P, AT, T], F32R) for n in range(2)]
        qk = placed(27648, "qk", [P, 2, AT, T])
        gst = placed(46080, "gst", [P, 2, T])
        xtok = placed(58880, "xtok", [P, 5, D])
        xsq = placed(58880 + 20480, "xsq", [P, D])
        hf = placed(58880 + 24576, "hf", [P, 2, 4, P])
        gnat = placed(50688, "gnat", [P, GP, CH, GC])
        up_ = placed(50688, "uchunk", [P, 2, 8, CH, GC])
        yb = placed(50688, "ychunk", [P, 2, CH, P])
        tm = [placed(58880 + 9216 * n, f"tm{n}", [P, GP, CH + 1, GC]) for n in range(2)]
        vs = placed(9216, "vs", [GC, G, P])
        UT = placed(58880, "UT", [P, G, NCH])
        uT = placed(0, "uT", [P, AT, T])
        Hb = placed(58880 + 9216, "Hb", [P, 2, GP, NCH])
        sc = [placed(50688, "sc0", [P, 2, GP, NPC - 1]), placed(0, "sc1", [P, 2, GP, NPC - 1])]
        CA = placed(77312, "CA", [P, 2, GP, CH + 1, GC])
        GT = placed(95744, "GT", [P, 2, GP, P])
        Tm = placed(95744, "Tm", [P, G, P])
        at = 112128

        def small(name, shape, dt=F32):
            nonlocal at
            t = placed(at, name, shape, dt)
            at += 4 * int(np.prod(shape[1:]))
            return t

        are, aim, ldt = (small(n, [P, GP]) for n in ("are", "aim", "ldt"))
        ta = [small(f"ta{n}", [P, GP]) for n in range(6)]
        pw_ = small("powers", [P, 2, CH + 1, GP])
        sq8 = small("sq8", [P, 2, 7, GP])
        t9 = [small(f"t9_{n}", [P, 2, GP, 9]) for n in range(2)]
        bnat = placed(0, "bnat", [P, 2, GP, GC])
        bb = small("bb", [P, 2, GP, GC])
        cnat = placed(2048, "cnat", [P, 2, 2, P])
        cT = small("cT", [P, 2, GP, GC])
        h0 = placed(19712, "h0", [P, 2, GP, SB])
        Fh = small("Fh", [P, 2, GP, 9])
        dd = small("dd", [GC, G])
        assert at <= 112128 + 10752, at
        sel = placed(9216, "sel", [16, 8, P])
        kst = placed(13312, "kst", [P, 2, AW])
        nrm = placed(17408, "nrm", [16, T])
        snat = placed(4096, "snat", [P, 2 * P])
        Fo = placed(20736, "Fo", [P, 2, 9 * GP])
        sst = placed(21888, "sst", [P, 2, 2 * P])
        dti = placed(25600, "dti", [GC, G, GC])
        vT = placed(9216, "vT", [P, AT, T])
        vtok = placed(50688, "vtok", [P, 5, AW])
        pr = [placed(60928 + 2048 * n, f"pr{n}", [P, TP], F32R) for n in range(6)]
        khi, klo, qhi, qlo, vhi, vlo = pr
        score = []
        for n, (at, w) in enumerate(((73216, SZW), (97792, ZW))):
            score.append([[placed(at + 4 * w * q, f"score{n}_{q}_{name}", [P, w], dt) for q in range(4)]
                          for name, dt in (("f", F32), ("r", F32R))])

        def t2(h):
            return score[h % 2][0][2 * (h // 2 % 2)]

        def t1(h):
            return score[h % 2][0][2 * (h // 2 % 2) + 1]

        def Wsp(h):
            q = 2 * (h // 2 % 2)
            return score[h % 2][1][q:q + 2]

        def Lsp(h):
            q = 2 - 2 * (h // 2 % 2)
            return score[h % 2][1][q:q + 2]

        brow = placed(118272, "brow", [1, SB * AT * 16])
        Qb = placed(120320, "Qb", [P, SB, AT, 16])
        KTb = placed(60928, "KTb", [P, 2, AW])
        vnew = [placed(at, f"vnew{n}", [ST, SB // 2, AW]) for n, at in enumerate((60928 + 4096, 85504))]
        pages = placed(97792, "pages", [P, NPAGE, AW])
        pti = placed(122368, "pti", [1, SB * NPG], I32)
        sbr = placed(122368 + 64, "sbr", [1, H])
        mg = [placed(46080 + 18432 * n, f"mg{n}", [P, KT, T], F32R) for n in range(2)]
        yh = [placed(27648 + 9216 * n, f"yh{n}", [P, AT, T], F32R) for n in range(2)]
        gl = placed(82944, "gl", [P, 2, 2, 2, T])
        mt = [placed(101376 + 4608 * n, f"mt{n}", [P, 2, T]) for n in range(3)]
        R = placed(0, "R", [P, KT, T])
        xtok2 = placed(115200, "xtok2", [P, 2, D])
        hid = [[placed(64512 + 18432 * b + 9216 * n, f"hid{b}{n}", [P, 4, T], F32R) for n in range(2)] for b in range(2)]
        sq = placed(101376, "sq", [P, 2, T])
        xf = placed(101376 + 4608, "xf", [P, 2, T])
        inv = placed(101376 + 9216, "inv", [P, T])
        hr = placed(101376 + 11520, "hr", [P, 2, T])
        hs = placed(101376 + 16128, "hs", [P, 2, T])
        dtmp = placed(101376 + 20736, "dtmp", [P, 2, T])
        pT = [placed(27648 + 4608 * n, f"pT{n}", [P, 2, T], F32R) for n in range(2)]
        ptok = placed(27648 + 9216, "ptok", [P, 2, PLE])
        pw = placed(27648 + 11264, "pw", [P, KT, T])
        ytok = placed(64512, "ytok", [P, 5, D])
        yf = placed(64512 + 20480, "yf", [P, 2, T])
        ysg = placed(64512 + 20480 + 4608, "ysg", [P, 2, T])

        banks = ctx.enter_context(nc.psum_tensor("banks", [P, 4, 512], F32))
        dense = ctx.enter_context(nc.psum_tensor("dense", [P, 2, 2, 512], F32))
        gates_d = nc.dram_tensor("gates_spill", [16, P, T], F32, kind="Internal").ap()
        vs_d = nc.dram_tensor("vs_spill", [GC, G, P], F32, kind="Internal").ap()

        def bank(job):
            if jobs[job][0] == LASTBANK:
                return dense[:, 1, 1, :]
            if jobs[job][0] >= DENSE:
                return dense[:, jobs[job][0] - DENSE, 0, :]
            return banks[:, jobs[job][0], :]

        def dplace(job):
            return dense[:, jobs[job][0] - DENSE]

        def prod(job):
            return dplace(job)[:, :, 0:HT]

        def halves(ap):
            return ap.rearrange("p (a n) -> p a n", a=2)

        def f32(ap):
            return ap.bitcast(F32)

        def wsrc(u):
            kind, m, nk, nm = units[u]
            name, row, col = {
                "q": ("w_in", 0, 0), "k": ("w_in", 0, AW), "v": ("w_in", 0, 2 * AW), "u": ("w_in", 0, 3 * AW),
                "gate": ("w_in", 0, 4 * AW), "attn": ("w_attn_out", 0, 0), "val": ("w_glu_val", 0, 0),
                "glu": ("w_glu_gate", 0, 0), "out": ("w_out", 0, 0), "up": ("w_up", 0, 0),
                "down": ("w_down", 512 * (m // 8), 0), "ple": ("w_ple", 0, 0), "pgate": ("w_ple_gate", 0, 0)}[kind]
            col += 128 * (m % 8 if kind == "down" else m)
            w = i[name][0][row:row + 128 * nk, col:col + 128 * nm]
            return w.rearrange("(k p) m -> p k m", p=P)

        def wview(t, slot, u):
            return t[:, slot, :].rearrange("p (k m) -> p k m", k=units[u][2])

        def last_job(u):
            return ("m", u, units[u][3] - 1)

        FIRST = {}
        for n, u in enumerate(units):
            FIRST.setdefault(u[0], n)

        def full_of(job):
            return psum_full[jobs[job][0]]

        def free_of(job):
            return psum_free[jobs[job][0]]

        def full(job):
            return full_of(job), jobs[job][1] + 1

        def read(job):
            return free_of(job), jobs[job][1] + 1

        def used_before(job):
            return jobs[job][1] > 0

        def free(job):
            return free_of(job), jobs[job][1]

        block = ctx.enter_context(nc.Block())

        @block.sync
        def _(sync):
            small_loads = [
                (gains[:, 0, :], i["g_mix"][0].rearrange("(k p) -> p k", p=P)),
                (gqk[0:HD, 0:1], i["g_q"].rearrange("a d -> d a")), (gqk[HD:P, 0:1], i["g_q"].rearrange("a d -> d a")),
                (gqk[0:HD, 1:2], i["g_k"].rearrange("a d -> d a")), (gqk[HD:P, 1:2], i["g_k"].rearrange("a d -> d a")),
                (are[:, :], i["ssm_a_re"][0].rearrange("(p g) s -> (g s) p", g=2)),
                (aim[:, :], i["ssm_a_im"][0].rearrange("(p g) s -> (g s) p", g=2)),
                (bnat[:, 0], i["ssm_b_re"][0].rearrange("(p g) s c -> (g s) p c", g=2)),
                (bnat[:, 1], i["ssm_b_im"][0].rearrange("(p g) s c -> (g s) p c", g=2)),
                (snat[:, :], i["state_ssm"][0].rearrange("b (p g) s i -> (b p) (g s i)", g=2)),
                (dd[:, :], i["ssm_d"][0].rearrange("(g c) -> c g", c=GC)),
                (gains[:, 1, :], i["g_mlp"][0].rearrange("(k p) -> p k", p=P)),
                (gains[:, 2, :], i["g_ple"][0].rearrange("(k p) -> p k", p=P)),
                (bias[:, :], i["sb_bias"][0:1, :].to_broadcast([P, H])),
            ]
            for g in range(2):
                small_loads.append((ldt[64 * g:64 * g + 64, :],
                                    i["ssm_log_dt"][0:1].rearrange("a (p g) -> a p g", g=2)[:, :, g].to_broadcast([64, GP])))
                for part, n in enumerate(("ssm_c_re", "ssm_c_im")):
                    for blk in range(2):
                        src = i[n][0][16 * blk:16 * blk + 16].rearrange("(p g) c s -> g p c s", g=2)[g]
                        small_loads.append((cnat[:, part, blk, 64 * g:64 * g + 64], src))

            def weights(u):
                if u >= NRAW:
                    sync.wait_ge(w_lo, u - NRAW + 1)
                dst = wview(wraw, u % NRAW, u)
                sync.dma_start(dst, wsrc(u)).then_inc(raw_in[u % NRAW], 16)

            def tokens(t):
                t0, n = TOK[t]
                src = i["x_prompt"][0][t0:t0 + n, :] if t < 4 else i["x_sample"].rearrange("b s d -> (b s) d")
                sync.dma_start(xtok[0:n, t, :], src).then_inc(x_in[t], 16)

            def load_page(n):
                j, cache = n % (SB * NPG), i["cache_k" if n < SB * NPG else "cache_v"]
                page = sync.value_load(pti[0:1, j:j + 1], min_val=0, max_val=cache.shape[1] - 1)
                sync.dma_start(pages[:, n % NPAGE, :],
                               cache[0][bass.ds(page, 1)].rearrange("a r h d -> (a r) (h d)")).then_inc(
                                   page_in[n % NPAGE], 16)

            for t in range(5):
                tokens(t)
            weights(0)
            for n, (dst, src) in enumerate(small_loads):
                sync.dma_start(dst, src, allow_slow_non_contiguous=True).then_inc(
                    gmix_in if n == 0 else params_in, 16)
            for u in range(1, len(units)):
                weights(u)
                if u == FIRST["v"] + AT + 5:
                    sync.wait_ge(table_in, 16)
                    sync.wait_ge(*full(("av", H - 1)))
                    for n in range(SB * NPG + NPAGE):
                        if n >= NPAGE:
                            sync.wait_ge(*full(("skt", n - NPAGE)))
                        load_page(n)
                if u == FIRST["v"] + AT + 9:
                    for n in range(SB * NPG + NPAGE, 2 * SB * NPG):
                        sync.wait_ge(vb_used, (n - SB * NPG - NPAGE) // NPG + 1)
                        load_page(n)

            for part in range(2):
                sync.wait_ge(*read(("yout", KT // 2 * (part + 1) - 1, "b")))
                cols = slice(D // 2 * part, D // 2 * part + D // 2)
                for t in range(5):
                    t0, n = TOK[t]
                    dst = o["y_prompt"][0][t0:t0 + n, cols] if t < 4 else o["y_sample"].rearrange("b s d -> (b s) d")[:, cols]
                    sync.dma_start(dst, ytok[0:n, t, cols]).then_inc(y_stored, 16)
            sync.wait_ge(y_stored, 16 * 10)

        N_PARAMS = 13 + 2 * 5

        @block.gpsimd
        def _(pool):
            count = Count()
            out_dmas = [0]

            def store(dst, src):
                pool.dma_start(dst, src).then_inc(stored, 16)
                out_dmas[0] += 1

            def tt(out, in0, in1, op):
                return nc.gpsimd.tensor_tensor(out=out, in0=in0, in1=in1, op=op)

            nc.gpsimd.memset(ident[:, :], 0.0).then_inc(count.up(pool_steps), 1)
            nc.gpsimd.memset(ones[:, :], 1.0).then_inc(count.up(pool_steps), 1)
            nc.gpsimd.memset(eps[:, :], EPS).then_inc(count.up(pool_steps), 1)
            nc.gpsimd.memset(halfpi[:, :], PI / 2).then_inc(count.up(pool_steps), 1)
            nc.gpsimd.memset(hsum[:, :, :], 0.0).then_inc(count.up(pool_steps), 1)
            pool.wait_ge(*count.last)
            nc.gpsimd.affine_select(out=ident[:, :], in_=ident[:, :], compare_op=ALU.not_equal, fill=1.0, base=0,
                                   pattern=[[-1, P]], channel_multiplier=1).then_inc(count.up(ident_ready), 1)
            hflat = hsum[:, :, :].rearrange("p a b -> p (a b)")
            pool.wait_ge(*count.last)
            nc.gpsimd.memset(hflat[0:64, 0:P:18], 1.0).then_inc(count.up(pool_steps), 1)
            pool.wait_ge(*count.last)
            nc.gpsimd.memset(hflat[64:P, 1:P:18], 1.0).then_inc(count.up(pool_steps), 1)
            pool.wait_ge(*count.last)
            mneg = gst[:, 0, 0:P]
            nc.gpsimd.memset(mneg, -1.0).then_inc(count.up(pool_steps), 1)
            pool.wait_ge(*count.last)
            nc.gpsimd.tensor_copy(negs[:, :], mneg).then_inc(count.up(pool_steps), 1)
            pool.wait_ge(*count.last)
            nc.gpsimd.affine_select(out=mneg, in_=mneg, compare_op=ALU.is_ge, fill=0.0, base=0,
                                   pattern=[[-1, P]], channel_multiplier=1).then_inc(count.up(pool_steps), 1)
            pool.wait_ge(*count.last)
            nc.gpsimd.tensor_copy(tri[:, :], mneg).then_inc(count.up(pool_steps), 1)
            sflat = sel[:, :, :].rearrange("r p c -> r (p c)")
            nc.gpsimd.memset(sflat, 1.0).then_inc(count.up(pool_steps), 1)
            pool.wait_ge(*count.last)
            nc.gpsimd.affine_select(out=sflat, in_=sflat, compare_op=ALU.is_ge, fill=0.0, base=0,
                                   pattern=[[1, 8 * P]], channel_multiplier=-64).then_inc(count.up(pool_steps), 1)
            pool.wait_ge(*count.last)
            nc.gpsimd.affine_select(out=sflat, in_=sflat, compare_op=ALU.is_ge, fill=0.0, base=63,
                                   pattern=[[-1, 8 * P]], channel_multiplier=64).then_inc(count.up(pool_steps), 1)
            pool.wait_ge(*count.last)
            nc.gpsimd.tensor_copy(stat[:, 2, 0:1], ident[:, 0:1]).then_inc(count.up(consts_ready), 1)

            def powers(lo, hi, n, part, step=1):
                v = pw_[:, part, lo:hi, :].rearrange("q k p -> q p k")
                if step < 0:
                    v = v[:, :, ::-1]
                return v.unsqueeze(3).to_broadcast([P, GP, n, GC])

            def gates_in(j):
                for slot in range(2):
                    pool.wait_ge(gate_out[slot], 16 * (j + 5))
                for which in range(2):
                    src = gates_d[8 * which + 2 * j:8 * which + 2 * j + 2].rearrange("m p t -> p m t")
                    pool.dma_start(gl[:, j % 2, which], src).then_inc(gl_in[j % 2], 16)

            def load_vnew(b):
                dst = vnew[2 * b // SB][:, b % (SB // 2), :]
                pool.dma_start(dst, vtok[ST * b:ST * b + ST, 4, :]).then_inc(vnew_in[b], 16)

            def load_x2(t):
                t0, n = TOK[t]
                src = i["x_prompt"][0][t0:t0 + n, :] if t < 4 else i["x_sample"].rearrange("b s d -> (b s) d")
                pool.dma_start(xtok2[0:n, t % 2, :], src).then_inc(x2_in[t % 2], 16)

            def load_p(t):
                t0, n = TOK[t]
                src = i["p_prompt"][0, 0][t0:t0 + n, :] if t < 4 else i["p_sample"][0].rearrange("b s d -> (b s) d")
                pool.dma_start(ptok[0:n, t % 2, :], src).then_inc(p_in[t % 2], 16)

            for e in schedule:
                k, a = e[0], e[1:]
                if k == "s5big" and a[0] == 0:
                    pool.wait_ge(s5_powers, 1)
                    pool.wait_ge(h_lo, 10)
                    cr, ci = [cT[:, n].unsqueeze(2).to_broadcast([P, GP, CH + 1, GC]) for n in range(2)]
                    prr, pri = [powers(0, CH + 1, CH + 1, n) for n in range(2)]
                    pool.wait_ge(*read("s5ct"))
                    tt(tm[0][:], prr, cr, ALU.mult).then_inc(count.up(pool_steps), 1)
                    tt(tm[1][:], pri, ci, ALU.mult).then_inc(count.up(pool_steps), 1)
                    pool.wait_ge(*count.last)
                    tt(CA[:, 0], tm[0][:], tm[1][:], ALU.subtract).then_inc(count.up(pool_steps), 1)
                    pool.wait_ge(*count.last)
                    tt(tm[0][:], prr, ci, ALU.mult).then_inc(count.up(pool_steps), 1)
                    tt(tm[1][:], pri, cr, ALU.mult).then_inc(count.up(pool_steps), 1)
                    pool.wait_ge(*count.last)
                    tt(tm[0][:], tm[0][:], tm[1][:], ALU.add).then_inc(count.up(pool_steps), 1)
                    pool.wait_ge(*count.last)
                    nc.gpsimd.tensor_scalar(CA[:, 1], tm[0][:], -1.0, None, ALU.mult).then_inc(count.up(ca_ready), 1)
                    pool.wait_ge(*count.last)
                if k == "s5big":
                    part = a[0]
                    br, bi = [bb[:, n].unsqueeze(2).to_broadcast([P, GP, CH, GC]) for n in range(2)]
                    pr_, pi_ = [powers(0, CH, CH, n, -1) for n in range(2)]
                    if part == 0:
                        pool.wait_ge(s5_bb, 1)
                    else:
                        pool.wait_ge(*full(("gt", 0, 2)))
                        pool.wait_ge(*full(("gt", 0, 3)))
                    tt(tm[0][:, :, 0:CH, :], pr_, br if part == 0 else bi, ALU.mult).then_inc(
                        count.up(pool_steps), 1)
                    tt(tm[1][:, :, 0:CH, :], pi_, bi if part == 0 else br, ALU.mult).then_inc(
                        count.up(pool_steps), 1)
                    pool.wait_ge(*count.last)
                    nc.gpsimd.tensor_tensor(out=gnat[:], in0=tm[0][:, :, 0:CH, :], in1=tm[1][:, :, 0:CH, :],
                                           op=ALU.subtract if part == 0 else ALU.add).then_inc(
                                               count.up(gnat_ready), 1)
                elif k == "vd":
                    tt(dti[:], ident[0:GC, 0:GC].unsqueeze(1).to_broadcast([GC, G, GC]),
                       dd[:].unsqueeze(2).to_broadcast([GC, G, GC]), ALU.mult).then_inc(count.up(pool_steps), 1)
                    pool.wait_ge(*count.last)
                    for n in (6, 7):
                        pool.wait_ge(*read(("vs", n)))
                    tt(vs[:, :, 0:GC], vs[:, :, 0:GC], dti[:], ALU.add).then_inc(count.up(vs_ready), 1)
                    pool.wait_ge(vs_ready, 1)
                    pool.dma_start(vs_d, vs[:]).then_inc(vs_spilled, 16)
                elif k == "kout":
                    t = a[0]
                    t0, n = TOK[t]
                    pool.wait_ge(*read(("kout", t)))
                    dst = (o["k_prompt"].rearrange("a b s h d -> (a b s) (h d)")[t0:t0 + n, :] if t < 4
                           else o["k_sample"].rearrange("a b s h d -> (a b s) (h d)"))
                    pool.dma_start(dst, kst[0:n, t % 2, :]).then_inc(k_stored[t % 2], 16)
                elif k == "tzero":
                    for p in range(2):
                        for n in range(4):
                            pool.wait_ge(*full(("s", n, p)))
                    nc.gpsimd.memset(Tm[:], 0.0).then_inc(count.up(tm_zero), 1)
                elif k == "tload":
                    pool.wait_ge(tm_zero, 1)
                    pool.wait_ge(vs_spilled, 16)
                    for n in range(CH):
                        pool.dma_start(Tm[GC * n:GC * n + GC, :, GC * n:P],
                                      vs_d[:, :, 0:P - GC * n]).then_inc(t_in, 16)
                elif k == "pairqk":
                    p = a[0]
                    if p:
                        pool.wait_ge(z_ready, 2 * p)
                    else:
                        pool.wait_ge(*full(("y", 3, 1)))
                        pool.wait_ge(fo_ready, 1)
                    nc.gpsimd.tensor_copy(khi[:], qk[:, 1, p, 0:TP]).then_inc(count.up(qk_hi), 1)
                    nc.gpsimd.tensor_copy(qhi[:], qk[:, 0, p, 0:TP]).then_inc(count.up(qk_hi), 1)
                    pool.wait_ge(*count.last)
                    tt(klo[:], qk[:, 1, p, 0:TP], f32(khi[:]), ALU.subtract).then_inc(count.up(qk_lo), 1)
                    tt(qlo[:], qk[:, 0, p, 0:TP], f32(qhi[:]), ALU.subtract).then_inc(count.up(qk_lo), 1)
                    if p == 0:
                        pool.dma_start(sbr[:, :], i["sb_bias"]).then_inc(brow_in, 16)
                        pool.dma_start(pti[:, :], i["page_table"].rearrange("b (n o) -> o (b n)", o=1)).then_inc(
                            table_in, 16)
                elif k == "sfinal":
                    pool.wait_ge(*read("sfinal"))
                    store(o["ssm_sample"].rearrange("a b (p g) s i -> (a b p) (g s i)", g=2), sst[:, 0, :])
                    store(o["ssm_prompt"].rearrange("a b (p g) s i -> (a b p) (g s i)", g=2), sst[0:GP, 1, :])
                elif k == "vout":
                    t = a[0]
                    t0, n = TOK[t]
                    pool.wait_ge(*read(("vout", t)))
                    store(o["v_prompt"].rearrange("a b s h d -> (a b s) (h d)")[t0:t0 + n, :] if t < 4
                          else o["v_sample"].rearrange("a b s h d -> (a b s) (h d)"), vtok[0:n, t, :])
                elif k == "unit" and units[a[0]][0] == "gate":
                    m = units[a[0]][1]
                    pool.wait_ge(*read(("m", a[0], 0)))
                    pool.dma_start(gates_d[m], gst[:, m % 2, :]).then_inc(gate_out[m % 2], 16)
                elif k == "zln" and a[0] < H:
                    pool.wait_ge(L_raw, a[0] + 1)
                    for b in range(4):
                        v = t2(a[0])[:, ZOFF[b]:ZOFF[b] + P]
                        nc.gpsimd.affine_select(out=v, in_=v, compare_op=ALU.is_gt, fill=0.0, base=0,
                                                pattern=[[1, P]], channel_multiplier=-1).then_inc(
                                                    count.up(L_masked), 1)
                elif k == "cum":
                    pool.wait_ge(z_free, a[0] + 1)
                    for b in range(4):
                        v = t1(a[0])[:, ZOFF[b]:ZOFF[b] + P]
                        nc.gpsimd.affine_select(out=v, in_=v, compare_op=ALU.is_gt, fill=0.0, base=0,
                                                pattern=[[1, P]], channel_multiplier=-1).then_inc(
                                                    count.up(w_masked), 1)
                elif k == "sz":
                    pool.wait_ge(*full(("av", H - 1)))
                    for b in range(SB // 2):
                        load_vnew(b)
                elif k == "zln":
                    pool.wait_ge(L_raw, H + 1)
                    v = t2(H)[0:ST, 1024:SZW].rearrange("p (c t) -> p c t", t=ST)
                    nc.gpsimd.affine_select(out=v, in_=v, compare_op=ALU.is_gt, fill=0.0, base=0,
                                            pattern=[[0, 64], [1, ST]], channel_multiplier=-1).then_inc(
                                                count.up(L_masked), 1)
                elif k == "scum":
                    pool.wait_ge(z_free, H + 1)
                    v = t1(H)[0:ST, 1024:SZW].rearrange("p (c t) -> p c t", t=ST)
                    nc.gpsimd.affine_select(out=v, in_=v, compare_op=ALU.is_gt, fill=0.0, base=0,
                                            pattern=[[0, 64], [1, ST]], channel_multiplier=-1).then_inc(
                                                count.up(w_masked), 1)
                elif k == "ysplit":
                    pool.wait_ge(cum_ready, H + 1)
                    for b in range(SB // 2, SB):
                        load_vnew(b)
                elif k == "merge":
                    pool.wait_ge(*full("sav"))
                    for j in range(2):
                        gates_in(j)
                    for t in range(2):
                        load_x2(t)
                elif k == "unit" and units[a[0]][0] == "glu":
                    j = units[a[0]][1] // 2
                    if j < 2:
                        pool.wait_ge(mg_done, j + 1)
                        gates_in(j + 2)
                elif k == "xT" and a[1] == 1 and a[0] < 3:
                    pool.wait_ge(*full(("xT", a[0], 1)))
                    load_x2(a[0] + 2)
                elif k == "unit" and units[a[0]][0] == "up" and units[a[0]][1] == 0:
                    pool.wait_ge(*full(("m", a[0] - 1, 0)))
                    for t in range(2):
                        load_p(t)
                elif k == "pT" and a[0] < 3:
                    pool.wait_ge(*full(("pT", a[0])))
                    load_p(a[0] + 2)

            pool.wait_ge(k_stored[0], 16 * 3)
            pool.wait_ge(k_stored[1], 16 * 2)
            pool.wait_ge(stored, 16 * out_dmas[0])

        def piece_list(h):
            return [(P, 0, ZW)] if h < H else [(P, 0, 1024), (ST, 1024, SZW)]

        def zflat(h, rows, c0, c1):
            if h % 2:
                return dense[0:rows, :, :, :].rearrange("p a b c -> p (a b c)")[:, c0:c1]
            return banks[0:rows, 0:3, :].rearrange("p b c -> p (b c)")[:, c0:c1]

        def sample_out(h2):
            v = bank("sav").rearrange("q (b p h t) -> q h p b t", b=SB, p=AT, h=2)
            return v[64 * h2:64 * h2 + 64, h2]

        def sample_cols(t, h2):
            return t[64 * h2:64 * h2 + 64, :, TP:T].rearrange("q p (b t) -> q p b t", t=ST)

        @block.scalar
        def _(scalar):
            count = Count()

            def split(u):
                if u >= len(units):
                    return
                scalar.wait_ge(raw_in[u % NRAW], 16 * (u // NRAW + 1))
                if u >= NSPLIT:
                    scalar.wait_ge(*full(last_job(u - NSPLIT)))
                nc.scalar.copy(whi[:, u % NSPLIT, :], wraw[:, u % NRAW, :]).then_inc(count.up(w_hi), 1)

            def feed(m, w):
                scalar.wait_ge(xf_ready, count.next(xf_ready))
                nc.scalar.copy(act[0][:, m, :], xf[:, m % 2, :]).then_inc(count.up(act_hi), 1)
                if m >= 2:
                    scalar.wait_ge(ms_used, (KT - 1) * (w - 1) + m - 1)
                elif w == 2:
                    scalar.wait_ge(*full(("ms", 0, "b")))
                nc.scalar.activation(sq[:, m % 2, :], R[:, m, :], ACT.Square).then_inc(count.up(ms_sq), 1)

            def unit_out(u):
                kind, m0, nk, nm = units[u]
                if kind == "attn":
                    j = m0 // 2
                    scalar.wait_ge(gl_in[j % 2], 32 * (j // 2 + 1))
                    nc.scalar.activation(gl[:, j % 2], gl[:, j % 2], ACT.Sigmoid).then_inc(count.up(gl_sig), 1)
                for j in range(nm):
                    job = ("m", u, j)
                    if kind in ("attn", "val"):
                        continue
                    m = m0 + j
                    if kind in "qk":
                        p = m + (AT if kind == "k" else 0)
                        scalar.wait_ge(*full(job))
                        if p > 1:
                            scalar.wait_ge(sq_used, p - 1)
                        nc.scalar.activation(halves(gst[:, p % 2, :]), prod(job), ACT.Square).then_inc(
                            count.up(sq_ready), 1)
                        nc.scalar.copy(halves(qk[:, p // AT, m, :]), prod(job)).then_inc(count.upto(*read(job)), 1)
                    elif kind == "u":
                        scalar.wait_ge(*full(job))
                        scalar.wait_ge(s5_bb, 1)
                        nc.scalar.copy(halves(uT[:, m, :]), prod(job)).then_inc(count.upto(*read(job)), 1)
                    elif kind == "v":
                        scalar.wait_ge(*full(job))
                        if m == 0:
                            scalar.wait_ge(k_stored[0], 16 * 3)
                            scalar.wait_ge(k_stored[1], 16 * 2)
                        nc.scalar.copy(halves(vT[:, m, :]), prod(job)).then_inc(count.upto(*read(job)), 1)
                    elif kind == "gate":
                        scalar.wait_ge(*full(job))
                        if m > 1:
                            scalar.wait_ge(gate_out[m % 2], 16 * (m // 2))
                        nc.scalar.copy(halves(gst[:, m % 2, :]), prod(job)).then_inc(count.upto(*read(job)), 1)
                    elif kind == "glu":
                        scalar.wait_ge(*full(job))
                        nc.scalar.activation(halves(mt[2][:, j, :]), prod(job), ACT.Sigmoid).then_inc(
                            count.upto(*read(job)), 1)
                    elif kind == "up":
                        scalar.wait_ge(*full(job))
                        nc.scalar.activation(halves(hr[:, m % 2, :]), prod(job), ACT.Relu).then_inc(
                            count.upto(*read(job)), 1)
                        scalar.wait_ge(hs_ready, count.next(hs_ready))
                        nc.scalar.copy(hid[m // 4 % 2][0][:, m % 4, :], hs[:, m % 2, :]).then_inc(count.up(hid_hi), 1)
                    elif kind == "out":
                        feed(m, 1)
                    elif kind == "down" and m0 // 8 == 7:
                        feed(m % 8, 2)
                    elif kind == "ple":
                        scalar.wait_ge(*full(job))
                        nc.scalar.copy(halves(pw[:, m, :]), prod(job)).then_inc(count.upto(*read(job)), 1)
                    elif kind == "pgate":
                        scalar.wait_ge(*read(job))
                        nc.scalar.activation(ysg[:, m % 2, :], yf[:, m % 2, :], ACT.Sigmoid).then_inc(
                            count.up(ysg_ready), 1)
                if kind == "glu":
                    if m0 == 0:
                        for slot in range(2):
                            scalar.wait_ge(gate_out[slot], 16 * 8)
                    for j in range(2):
                        scalar.wait_ge(mg_ready, count.next(mg_ready))
                        nc.scalar.copy(mg[0][:, m0 + j, :], mt[0][:, j, :]).then_inc(count.up(mg_hi), 1)

            for e in schedule:
                k, a = e[0], e[1:]
                if k == "norm":
                    t = a[0]
                    t0, n = TOK[t]
                    scalar.wait_ge(x_in[t], 16)
                    if t:
                        scalar.wait_ge(*count.last)
                    nc.scalar.activation(xsq[0:n, :], xtok[0:n, t, :], ACT.Square,
                                         accum_out=stat[0:n, 0, t:t + 1]).then_inc(count.up(act_steps), 1)
                    scalar.wait_ge(*count.last)
                    if t == 0:
                        scalar.wait_ge(consts_ready, 1)
                    nc.scalar.activation(stat[0:n, 0, t:t + 1], stat[0:n, 0, t:t + 1], ACT.Sqrt, scale=1.0 / D,
                                         bias=eps[0:n, :]).then_inc(count.up(sd_ready), 1)
                elif k == "h":
                    t, half = a
                    t0, n = TOK[t]
                    scalar.wait_ge(*read(("h", t, half)))
                    nc.scalar.copy(act[0][:, 4 * half:4 * half + 4, t0:t0 + n], hf[:, half, :, 0:n]).then_inc(
                        count.up(h_hi), 1)
                elif k == "split0":
                    split(a[0])
                elif k == "s5small":
                    scalar.wait_ge(params_in, 16 * N_PARAMS)
                    nc.scalar.activation(ta[0][:], ldt[:], ACT.Exp).then_inc(count.up(dt_ready), 1)
                    scalar.wait_ge(theta_ready, 1)
                    nc.scalar.activation(ta[4][:], ta[1][:], ACT.Exp).then_inc(count.up(act_steps), 1)
                    nc.scalar.activation(ta[5][:], ta[2][:], ACT.Sin).then_inc(count.up(act_steps), 1)
                    nc.scalar.activation(ta[0][:], ta[2][:], ACT.Abs).then_inc(count.up(act_steps), 1)
                    scalar.wait_ge(*count.last)
                    nc.scalar.activation(ta[3][:], ta[0][:], ACT.Sin, scale=-1.0, bias=halfpi[:, :]).then_inc(
                        count.up(trig_ready), 1)
                elif k == "unit":
                    unit_out(a[0])
                    split(a[0] + NSPLIT)
                elif k == "qkrstd":
                    for half in range(2):
                        scalar.wait_ge(*full(f"qs{half}"))
                        nc.scalar.activation(nrm[:, HT * half:HT * half + HT], banks[0:16, half, 0:HT], ACT.Sqrt,
                                                 scale=1.0 / HD, bias=eps[0:16, :]).then_inc(
                                                     count.upto(*read(f"qs{half}")), 1)
                elif k in ("kout", "vout"):
                    t = a[0]
                    t0, n = TOK[t]
                    scalar.wait_ge(*full(e))
                    if k == "kout":
                        if t > 1:
                            scalar.wait_ge(k_stored[t % 2], 16 * (t // 2))
                    dst = kst[0:n, t % 2, :] if k == "kout" else vtok[0:n, t, :]
                    nc.scalar.copy(dst, bank(e)[0:n, :]).then_inc(count.upto(*read(e)), 1)
                elif k == "vs":
                    scalar.wait_ge(*full(e))
                    if a[0] == 0:
                        scalar.wait_ge(k_stored[0], 16 * 3)
                        scalar.wait_ge(k_stored[1], 16 * 2)
                    g0 = 8 * (a[0] // 2)
                    nc.scalar.copy(vs[:, g0 + a[0] % 2:g0 + 8:2, :],
                                   bank(e)[0:GC, :].rearrange("p (a b) -> p a b", a=4)).then_inc(
                                       count.upto(*read(e)), 1)
                elif k == "ut":
                    q, half = a
                    scalar.wait_ge(*full(e))
                    if q >= 2:
                        scalar.wait_ge(*full(("ug", q - 2, 1)))
                    nc.scalar.copy(up_[0:NCH, q % 2, :, 4 * half:4 * half + 4, :].rearrange("n g j c -> n j g c"),
                                       bank(e)[0:NCH, :].rearrange("n (j g c) -> n j g c", j=4, g=8)).then_inc(
                                           count.upto(*read(e)), 1)
                elif k == "sfinal":
                    scalar.wait_ge(*full(e[0]))
                    nc.scalar.activation(sst[:, 0, :].rearrange("r (q i) -> r i q", i=2),
                                         banks[:, 0, 0:2 * P].rearrange("r (i q) -> r i q", i=2), ACT.Copy).then_inc(
                        count.up(act_steps), 1)
                    nc.scalar.copy(sst[0:GP, 1, :].rearrange("r (q i) -> r i q", i=2),
                                       banks[0:GP, 0, 2 * P:4 * P].rearrange("r (i q) -> r i q", i=2)).then_inc(
                                           count.upto(*read(e[0])), 1)
                elif k == "y":
                    q, half = a
                    scalar.wait_ge(*full(e))
                    if q >= 2:
                        scalar.wait_ge(*full(("yt", q - 2, 1)))
                    nc.scalar.copy(yb[0:NCH, q % 2].rearrange("n j (g c) -> n g j c", c=GC)[:, half::2],
                                       bank(e)[0:NCH, :].rearrange("n (g j c) -> n g j c", g=4, j=CH)).then_inc(
                                           count.upto(*read(e)), 1)
                elif k == "yt":
                    q, half = a
                    scalar.wait_ge(*full(e))
                    dst = yact[:, q, :].rearrange("p (n j) -> p j n", j=CH)[:, 4 * half:4 * half + 4, :]
                    nc.scalar.activation(dst, bank(e)[:, 0:4 * NCH].rearrange("p (j n) -> p j n", j=4),
                                             ACT.Gelu_apprx_tanh).then_inc(count.upto(*read(e)), 1)
                elif k == "pairqk" and a[0] == 0:
                    nc.scalar.preload_act_table_set("natural_log_exp_and_others")
                elif k == "pairv":
                    p = a[0]
                    if p:
                        scalar.wait_ge(*full(("av", 2 * p - 1)))
                    nc.scalar.copy(vhi[:].rearrange("s (b c) -> s b c", b=4),
                                   vtok[:, 0:4, P * p:P * p + P]).then_inc(count.up(v_hi), 1)
                elif k == "zln":
                    h = a[0]
                    t = t1(h)
                    scalar.wait_ge(z_abs, h + 1)
                    for rows, c0, c1 in piece_list(h):
                        nc.scalar.activation(t[0:rows, c0:c1], t[0:rows, c0:c1], ACT.Exp).then_inc(
                            count.up(act_steps), 1)
                    scalar.wait_ge(*count.last)
                    for rows, c0, c1 in piece_list(h):
                        nc.scalar.activation(t[0:rows, c0:c1], t[0:rows, c0:c1], ACT.Ln, bias=1.0).then_inc(
                            count.up(l_ready if c1 > 1024 else act_steps), 1)
                elif k == "lsplit":
                    h = a[0]
                    scalar.wait_ge(L_masked, 4 * h + 4 if h < H else 4 * H + 1)
                    if h >= 2:
                        scalar.wait_ge(*full(("av", h - 2)))
                    for rows, c0, c1 in piece_list(h):
                        nc.scalar.copy(Lsp(h)[0][0:rows, c0:c1], t2(h)[0:rows, c0:c1]).then_inc(
                            count.up(L_hi if c1 > 1024 else act_steps), 1)
                elif k in ("cum", "scum"):
                    h = a[0] if k == "cum" else H
                    scalar.wait_ge(cum_ready, h + 1)
                    kw = {"bias": bias[:, h:h + 1]} if h < H else {}
                    for rows, c0, c1 in piece_list(h):
                        nc.scalar.activation(t1(h)[0:rows, c0:c1], zflat(h, rows, c0, c1), ACT.Exp, **kw).then_inc(
                            count.up(z_free if c1 > 1024 else act_steps), 1)
                elif k == "wsplit":
                    h = a[0]
                    scalar.wait_ge(w_masked, 4 * h + 4)
                    nc.scalar.copy(Wsp(h)[0][:, 0:ZW], t1(h)[:, 0:ZW]).then_inc(count.up(W_hi), 1)
                elif k == "oout":
                    h = a[0]
                    r = 64 * (h % 2)
                    scalar.wait_ge(*full(("av", h)))
                    nc.scalar.copy(oT[0][r:r + 64, h // 2, 0:TP], bank(("av", h))[r:r + 64, :]).then_inc(
                        count.up(o_hi), 1)
                elif k == "skt":
                    j = a[0]
                    scalar.wait_ge(*full(e))
                    if j > 1:
                        scalar.wait_ge(kt_used, j - 1)
                    nc.scalar.copy(KTb[:, j % 2, :], dplace(e)[:, 0, :]).then_inc(count.upto(*read(e)), 1)
                elif k == "sav" and a[0] == 3:
                    scalar.wait_ge(*full("sav"))
                    for h2 in range(2):
                        nc.scalar.copy(sample_cols(oT[0], h2), sample_out(h2)).then_inc(count.up(o_hi), 1)
                elif k == "ysplit":
                    nc.scalar.copy(yh[0][:], yact[:]).then_inc(count.up(y_hi), 1)
                elif k == "xT":
                    t, half = a
                    t0, n = TOK[t]
                    scalar.wait_ge(*full(e))
                    nc.scalar.copy(R[:, 4 * half:4 * half + 4, t0:t0 + n],
                                       dplace(e)[:, 0, :].rearrange("p (k n) -> p k n", k=4)[:, :, 0:n]).then_inc(
                                           count.upto(*read(e)), 1)
                elif k == "msinv" and a[0] == 1:
                    for half, ab in enumerate("ab"):
                        scalar.wait_ge(*full(("ms", 1, ab)))
                        nc.scalar.activation(inv[:, HT * half:HT * half + HT], banks[:, half, 0:HT], ACT.Sqrt,
                                                 scale=1.0 / D, bias=eps[:, :]).then_inc(
                                                     count.upto(*read(("ms", 1, ab))), 1)
                elif k == "pT":
                    t = a[0]
                    t0, n = TOK[t]
                    scalar.wait_ge(*full(e))
                    nc.scalar.copy(pT[0][:, :, t0:t0 + n], bank(e)[:, 0:2 * P].rearrange("p (k n) -> p k n", k=2)[:, :, 0:n]).then_inc(
                        count.up(pT_hi), 1)
                elif k == "yout":
                    m = a[0]
                    scalar.wait_ge(*full(("yout", m, "a")))
                    nc.scalar.copy(ytok[:, 0:4, P * m:P * m + P], banks[:, 2, :].rearrange("p (t c) -> p t c", t=4)).then_inc(
                        count.upto(*read(("yout", m, "a"))), 1)
                    scalar.wait_ge(*full(("yout", m, "b")))
                    nc.scalar.copy(ytok[0:TS, 4, P * m:P * m + P], banks[0:TS, 3, 0:P]).then_inc(
                        count.upto(*read(("yout", m, "b"))), 1)

        @block.vector
        def _(vector):
            count = Count()

            def tt(out, in0, in1, op):
                return nc.vector.tensor_tensor(out=out, in0=in0, in1=in1, op=op)

            def cmul(out_re, out_im, a_re, a_im, b_re, b_im, s1, s2):
                tt(out=s1, in0=a_re, in1=b_re, op=ALU.mult).then_inc(count.up(dve_steps), 1)
                tt(out=s2, in0=a_im, in1=b_im, op=ALU.mult).then_inc(count.up(dve_steps), 1)
                vector.wait_ge(*count.last)
                tt(out=out_re, in0=s1, in1=s2, op=ALU.subtract).then_inc(count.up(dve_steps), 1)
                vector.wait_ge(*count.last)
                tt(out=s1, in0=a_re, in1=b_im, op=ALU.mult).then_inc(count.up(dve_steps), 1)
                tt(out=s2, in0=a_im, in1=b_re, op=ALU.mult).then_inc(count.up(dve_steps), 1)
                vector.wait_ge(*count.last)
                tt(out=out_im, in0=s1, in1=s2, op=ALU.add).then_inc(count.up(dve_steps), 1)
                vector.wait_ge(*count.last)

            def lower(lo, whole, hi):
                return nc.vector.tensor_tensor(out=lo, in0=whole, in1=f32(hi), op=ALU.subtract)

            def split(u):
                if u < len(units):
                    vector.wait_ge(w_hi, u + 1)
                    lower(wlo[:, u % NSPLIT, :], wraw[:, u % NRAW, :], whi[:, u % NSPLIT, :]).then_inc(
                        count.up(w_lo), 1)

            def feed(m, w):
                vector.wait_ge(*count.last)
                nc.vector.tensor_scalar(xf[:, m % 2, :], R[:, m, :], gains[:, w, m:m + 1], None, ALU.mult).then_inc(
                    count.up(xf_ready), 1)

            def feed_low(m, w):
                vector.wait_ge(act_hi, KT * (w - 1) + m + 1)
                lower(act[1][:, m, :], xf[:, m % 2, :], act[0][:, m, :]).then_inc(count.up(act_lo), 1)

            def unit_out(u):
                kind, m0, nk, nm = units[u]
                for j in range(nm):
                    job = ("m", u, j)
                    m = m0 + j
                    if kind == "attn":
                        if j == 0:
                            vector.wait_ge(gl_sig, count.next(gl_sig))
                            if m == 0:
                                vector.wait_ge(stored, 16 * 7)
                        vector.wait_ge(*full(job))
                        nc.vector.tensor_tensor(out=halves(mt[0][:, j, :]), in0=halves(gl[:, m0 // 2 % 2, 0, j, :]),
                                                   in1=prod(job), op=ALU.mult).then_inc(count.upto(*read(job)), 1)
                    elif kind == "val":
                        vector.wait_ge(*full(job))
                        nc.vector.tensor_tensor(out=halves(mt[1][:, j, :]), in0=halves(gl[:, m0 // 2 % 2, 1, j, :]),
                                                   in1=prod(job), op=ALU.mult).then_inc(count.upto(*read(job)), 1)
                    elif kind == "glu":
                        vector.wait_ge(*read(job))
                        vector.wait_ge(*count.last)
                        tt(mt[1][:, j, :], mt[1][:, j, :], mt[2][:, j, :], ALU.mult).then_inc(
                            count.up(dve_steps), 1)
                        vector.wait_ge(*count.last)
                        tt(mt[0][:, j, :], mt[0][:, j, :], mt[1][:, j, :], ALU.add).then_inc(
                            count.up(mg_ready), 1)
                    elif kind == "up":
                        vector.wait_ge(*read(job))
                        tt(hs[:, m % 2, :], hr[:, m % 2, :], hr[:, m % 2, :], ALU.mult).then_inc(
                            count.up(hs_ready), 1)
                        vector.wait_ge(hid_hi, m + 1)
                        b = m // 4 % 2
                        lower(hid[b][1][:, m % 4, :], hs[:, m % 2, :], hid[b][0][:, m % 4, :]).then_inc(
                            count.up(hid_lo), 1)
                    elif kind == "out":
                        vector.wait_ge(*full(job))
                        nc.vector.tensor_tensor(out=halves(R[:, m, :]), in0=halves(R[:, m, :]), in1=prod(job),
                                                   op=ALU.add).then_inc(count.upto(*read(job)), 1)
                        feed(m, 1)
                        feed_low(m, 1)
                    elif kind == "down":
                        vector.wait_ge(*full(job))
                        nc.vector.tensor_tensor(out=halves(dtmp[:, m % 2, :]), in0=halves(inv[:]), in1=prod(job),
                                                   op=ALU.mult).then_inc(count.upto(*read(job)), 1)
                        vector.wait_ge(*count.last)
                        tt(R[:, m % 8, :], R[:, m % 8, :], dtmp[:, m % 2, :], ALU.add).then_inc(
                            count.up(dve_steps), 1)
                    elif kind == "pgate":
                        vector.wait_ge(*full(job))
                        if m >= 2:
                            vector.wait_ge(*full(("yout", m - 2, "b")))
                        nc.vector.tensor_tensor(out=halves(yf[:, m % 2, :]), in0=halves(inv[:]), in1=prod(job),
                                                   op=ALU.mult).then_inc(count.upto(*read(job)), 1)
                        vector.wait_ge(ysg_ready, count.next(ysg_ready))
                        tt(yf[:, m % 2, :], ysg[:, m % 2, :], pw[:, m, :], ALU.mult).then_inc(
                            count.up(dve_steps), 1)
                        vector.wait_ge(*count.last)
                        tt(yf[:, m % 2, :], yf[:, m % 2, :], R[:, m, :], ALU.add).then_inc(count.up(yf_ready), 1)
                if kind == "down" and m0 // 8 == 7:
                    for j in range(nm):
                        feed((m0 + j) % 8, 2)
                    for j in range(nm):
                        feed_low((m0 + j) % 8, 2)
                if kind == "glu":
                    for j in range(2):
                        vector.wait_ge(mg_hi, count.next(mg_hi))
                        lower(mg[1][:, m0 + j, :], mt[0][:, j, :], mg[0][:, m0 + j, :]).then_inc(
                            count.up(mg_lo), 1)
                    tt(stat[:, 1, 0:1], eps[:, :], eps[:, :], ALU.add).then_inc(count.up(mg_done), 1)
                    vector.wait_ge(*count.last)

            for e in schedule:
                k, a = e[0], e[1:]
                if k == "norm":
                    t = a[0]
                    n = TOK[t][1]
                    vector.wait_ge(sd_ready, t + 1)
                    nc.vector.reciprocal(stat[0:n, 1, t:t + 1], stat[0:n, 0, t:t + 1]).then_inc(
                        count.up(dve_steps), 1)
                    vector.wait_ge(*count.last)
                    nc.vector.tensor_scalar(xtok[0:n, t, :], xtok[0:n, t, :], stat[0:n, 1, t:t + 1], None,
                                            ALU.mult).then_inc(count.up(xn_ready), 1)
                elif k == "h":
                    t, half = a
                    t0, n = TOK[t]
                    vector.wait_ge(*full(e))
                    if t == 0:
                        vector.wait_ge(gmix_in, 16)
                    if t:
                        vector.wait_ge(h_lo, 2 * t)
                    nc.vector.tensor_tensor(out=hf[:, half, :, 0:n],
                                               in0=gains[:, 0, 4 * half:4 * half + 4].unsqueeze(2).to_broadcast([P, 4, n]),
                                               in1=bank(e).rearrange("p (k n) -> p k n", k=4)[:, :, 0:n], op=ALU.mult).then_inc(
                                                   count.upto(*read(e)), 1)
                elif k == "hlo":
                    t = a[0]
                    t0, n = TOK[t]
                    for half in range(2):
                        vector.wait_ge(h_hi, 2 * t + half + 1)
                        lower(act[1][:, 4 * half:4 * half + 4, t0:t0 + n], hf[:, half, :, 0:n],
                              act[0][:, 4 * half:4 * half + 4, t0:t0 + n]).then_inc(count.up(h_lo), 1)
                elif k == "split0":
                    split(a[0])
                elif k == "s5small":
                    vector.wait_ge(params_in, 16 * N_PARAMS)
                    nc.vector.tensor_scalar(gqk[:, 0:1], gqk[:, 0:1], HD ** -0.5, None, ALU.mult).then_inc(
                        count.up(dve_steps), 1)
                    nc.vector.memset(pw_[:, 0, 0, :], 1.0).then_inc(count.up(dve_steps), 1)
                    nc.vector.memset(pw_[:, 1, 0, :], 0.0).then_inc(count.up(dve_steps), 1)
                    vector.wait_ge(dt_ready, 1)
                    tt(ta[1][:], are[:], ta[0][:], ALU.mult).then_inc(count.up(dve_steps), 1)
                    tt(ta[2][:], aim[:], ta[0][:], ALU.mult).then_inc(count.up(dve_steps), 1)
                    vector.wait_ge(*count.last)
                    nc.vector.tensor_scalar(ta[3][:], ta[2][:], 1.0 / (2 * PI), MAGIC, ALU.mult, ALU.add).then_inc(
                        count.up(dve_steps), 1)
                    vector.wait_ge(*count.last)
                    nc.vector.tensor_scalar(ta[3][:], ta[3][:], MAGIC, None, ALU.subtract).then_inc(
                        count.up(dve_steps), 1)
                    vector.wait_ge(*count.last)
                    for c in (C1, C2, C3):
                        nc.vector.scalar_tensor_tensor(out=ta[2][:], in0=ta[3][:], scalar=-c, in1=ta[2][:],
                                                      op0=ALU.mult, op1=ALU.add).then_inc(count.up(dve_steps), 1)
                        vector.wait_ge(*count.last)
                    lim = 3.1415925
                    nc.vector.tensor_scalar(ta[2][:], ta[2][:], lim, -lim, ALU.min, ALU.max).then_inc(
                        count.up(theta_ready), 1)
                    vector.wait_ge(trig_ready, 1)
                    tt(pw_[:, 0, 1, :], ta[4][:], ta[3][:], ALU.mult).then_inc(count.up(dve_steps), 1)
                    tt(pw_[:, 1, 1, :], ta[4][:], ta[5][:], ALU.mult).then_inc(count.up(dve_steps), 1)
                    vector.wait_ge(*count.last)
                    for n in (1, 2, 4):
                        an = [pw_[:, q, n, :].unsqueeze(1).to_broadcast([P, n, GP]) for q in range(2)]
                        dst = [pw_[:, q, n + 1:2 * n + 1, :] for q in range(2)]
                        src = [pw_[:, q, 1:n + 1, :] for q in range(2)]
                        s1, s2 = [t9[q][:].rearrange("p a b c -> p (a b c)")[:, 0:n * GP].rearrange("p (n g) -> p n g", g=GP)
                                  for q in range(2)]
                        cmul(dst[0], dst[1], src[0], src[1], an[0], an[1], s1, s2)
                    for q in range(2):
                        nc.vector.tensor_copy(sq8[:, q, 0, :], pw_[:, q, 8, :]).then_inc(count.up(dve_steps), 1)
                    vector.wait_ge(*count.last)
                    for n in range(5):
                        c = [sq8[:, q, n, :] for q in range(2)]
                        cmul(sq8[:, 0, n + 1, :], sq8[:, 1, n + 1, :], c[0], c[1], c[0], c[1],
                             ta[0][:], ta[1][:])
                    nc.vector.tensor_scalar(ta[2][:], pw_[:, 0, 1, :], -1.0, None, ALU.add).then_inc(
                        count.up(s5_powers), 1)
                    tt(ta[0][:], are[:], are[:], ALU.mult).then_inc(count.up(dve_steps), 1)
                    tt(ta[1][:], aim[:], aim[:], ALU.mult).then_inc(count.up(dve_steps), 1)
                    vector.wait_ge(*count.last)
                    tt(ta[0][:], ta[0][:], ta[1][:], ALU.add).then_inc(count.up(dve_steps), 1)
                    vector.wait_ge(*count.last)
                    nc.vector.reciprocal(ta[0][:], ta[0][:]).then_inc(count.up(dve_steps), 1)
                    tt(ta[3][:], ta[2][:], are[:], ALU.mult).then_inc(count.up(dve_steps), 1)
                    tt(ta[4][:], pw_[:, 1, 1, :], aim[:], ALU.mult).then_inc(count.up(dve_steps), 1)
                    vector.wait_ge(*count.last)
                    tt(ta[3][:], ta[3][:], ta[4][:], ALU.add).then_inc(count.up(dve_steps), 1)
                    vector.wait_ge(*count.last)
                    tt(ta[4][:], pw_[:, 1, 1, :], are[:], ALU.mult).then_inc(count.up(dve_steps), 1)
                    tt(ta[5][:], ta[2][:], aim[:], ALU.mult).then_inc(count.up(dve_steps), 1)
                    vector.wait_ge(*count.last)
                    tt(ta[4][:], ta[4][:], ta[5][:], ALU.subtract).then_inc(count.up(dve_steps), 1)
                    vector.wait_ge(*count.last)
                    tt(ta[3][:], ta[3][:], ta[0][:], ALU.mult).then_inc(count.up(dve_steps), 1)
                    tt(ta[4][:], ta[4][:], ta[0][:], ALU.mult).then_inc(count.up(dve_steps), 1)
                    vector.wait_ge(*count.last)
                    f = [ta[3 + q][:].unsqueeze(2).to_broadcast([P, GP, GC]) for q in range(2)]
                    s1, s2 = [t9[q][:].rearrange("p a b c -> p (a b c)")[:, 0:GP * GC].rearrange("p (a c) -> p a c", c=GC)
                              for q in range(2)]
                    cmul(bb[:, 0], bb[:, 1], f[0], f[1], bnat[:, 0], bnat[:, 1], s1, s2)
                    nc.vector.memset(stat[:, 2, 1:2], 0.0).then_inc(count.up(s5_bb), 1)
                elif k == "s5ct":
                    vector.wait_ge(*full("s5ct"))
                    nc.vector.tensor_copy(cT[:].rearrange("p a b c -> p (a b c)"), bank("s5ct")).then_inc(
                        count.upto(*read("s5ct")), 1)
                elif k == "s5h0":
                    vector.wait_ge(*full("s5h0"))
                    nc.vector.tensor_copy(h0[:], bank("s5h0")[:, 0:2 * P].rearrange("q (i b p) -> q i p b", i=2, b=SB)).then_inc(
                        count.upto(*read("s5h0")), 1)
                elif k == "unit":
                    unit_out(a[0])
                    split(a[0] + NSPLIT)
                elif k == "qkrstd":
                    vector.wait_ge(*read("qs0"))
                    vector.wait_ge(*read("qs1"))
                    nc.vector.reciprocal(nrm[:], nrm[:]).then_inc(count.up(nrm_ready), 1)
                elif k == "qknorm":
                    p, half = a
                    vector.wait_ge(*full(e))
                    x = qk[:, p // AT, p % AT, HT * half:HT * half + HT]
                    nc.vector.scalar_tensor_tensor(out=x, in0=x, scalar=gqk[:, p // AT:p // AT + 1],
                                                      in1=bank(e)[:, 0:HT], op0=ALU.mult, op1=ALU.mult).then_inc(
                                                          count.upto(*read(e)), 1)
                elif k == "gt":
                    part, n = a
                    vector.wait_ge(*full(e))
                    nc.vector.tensor_copy(GT[:, part, 4 * n:4 * n + 4, :].rearrange("p a b -> p (a b)"), bank(e)).then_inc(
                        count.upto(*read(e)), 1)
                elif k == "ug":
                    q, half = a
                    vector.wait_ge(*full(e))
                    vector.wait_ge(gnat_ready, 2)
                    nc.vector.tensor_copy(UT[:, 8 * q + 4 * half:8 * q + 4 * half + 4, :].rearrange("p g n -> p (g n)"),
                                             bank(e)[:, 0:4 * NCH]).then_inc(count.upto(*read(e)), 1)
                elif k == "s":
                    n, part = a
                    vector.wait_ge(*full(e))
                    if n == 0 and part == 0:
                        nc.vector.memset(Hb[:, :, :, 0:1], 0.0).then_inc(count.up(dve_steps), 1)
                        nc.vector.tensor_copy(Hb[:, :, :, NPC:NCH], h0[:]).then_inc(count.up(dve_steps), 1)
                    src = bank(e)[:, 0:4 * NCH].rearrange("p (a n) -> p a n", a=4)
                    nc.vector.tensor_copy(Hb[:, part, 4 * n:4 * n + 4, 1:NPC], src[:, :, 0:NPC - 1]).then_inc(
                        count.up(dve_steps), 1)
                    nc.vector.tensor_copy(Fh[:, part, 4 * n:4 * n + 4, :], src[:, :, NPC - 1:NCH]).then_inc(
                        count.upto(*read(e)), 1)
                elif k == "scan":
                    lvl = a[0]
                    d = 1 << lvl
                    n = NPC - 1 - d
                    vector.wait_ge(*count.last)
                    src = Hb[:, :, :, 1:1 + n]
                    for q in range(2):
                        c = sq8[:, q, lvl, :].unsqueeze(1).unsqueeze(3).to_broadcast([P, 2, GP, n])
                        tt(sc[q][:, :, :, 0:n], src, c, ALU.mult).then_inc(count.up(dve_steps), 1)
                    vector.wait_ge(*count.last)
                    dst = Hb[:, :, :, 1 + d:NPC]
                    tt(dst, dst, sc[0][:, :, :, 0:n], ALU.add).then_inc(count.up(dve_steps), 1)
                    vector.wait_ge(*count.last)
                    tt(dst[:, 0], dst[:, 0], sc[1][:, 1, :, 0:n], ALU.subtract).then_inc(count.up(dve_steps), 1)
                    tt(dst[:, 1], dst[:, 1], sc[1][:, 0, :, 0:n], ALU.add).then_inc(count.up(scanned), 1)
                elif k == "sfinal":
                    vector.wait_ge(*count.last)
                    src = Hb[:, :, :, NPC - 1:NCH]
                    for q in range(2):
                        c = sq8[:, q, 0, :].unsqueeze(1).unsqueeze(3).to_broadcast([P, 2, GP, 9])
                        tt(t9[q][:], src, c, ALU.mult).then_inc(count.up(dve_steps), 1)
                    vector.wait_ge(*count.last)
                    tt(Fh[:], Fh[:], t9[0][:], ALU.add).then_inc(count.up(dve_steps), 1)
                    vector.wait_ge(*count.last)
                    tt(Fh[:, 0], Fh[:, 0], t9[1][:, 1], ALU.subtract).then_inc(count.up(dve_steps), 1)
                    tt(Fh[:, 1], Fh[:, 1], t9[1][:, 0], ALU.add).then_inc(count.up(dve_steps), 1)
                    vector.wait_ge(*count.last)
                    vector.wait_ge(vs_spilled, 16)
                    nc.vector.tensor_copy(Fo[:].rearrange("q i (n p) -> q i p n", p=GP), Fh[:]).then_inc(
                        count.up(fo_ready), 1)
                elif k == "pairv":
                    p = a[0]
                    vector.wait_ge(v_hi, p + 1)
                    vv = [x[:].rearrange("s (b c) -> s b c", b=4) for x in (vlo, vhi)]
                    lower(vv[0], vtok[:, 0:4, P * p:P * p + P], vv[1]).then_inc(count.up(v_lo), 1)
                elif k in ("z", "sl"):
                    h = a[0] if k == "z" else H
                    vector.wait_ge(*((z_ready, h + 1) if h < H else (kt_used, SB * NPG)))
                    for rows, c0, c1 in piece_list(h):
                        b = bias[0:rows, h:h + 1] if h < H else 0.0
                        nc.vector.tensor_scalar(t2(h)[0:rows, c0:c1], zflat(h, rows, c0, c1), b, None,
                                                ALU.add).then_inc(count.up(z_copied if c1 > 1024 else dve_steps), 1)
                    vector.wait_ge(z_copied, h + 1)
                    for rows, c0, c1 in piece_list(h):
                        z = t2(h)[0:rows, c0:c1]
                        nc.vector.scalar_tensor_tensor(out=t1(h)[0:rows, c0:c1], in0=z, scalar=-1.0, in1=z,
                                                       op0=ALU.mult, op1=ALU.min).then_inc(
                            count.up(z_abs if c1 > 1024 else dve_steps), 1)
                elif k == "zln":
                    h = a[0]
                    ta_, tb = t1(h), t2(h)
                    vector.wait_ge(l_ready, h + 1)
                    for rows, c0, c1 in piece_list(h):
                        nc.vector.scalar_tensor_tensor(out=tb[0:rows, c0:c1], in0=tb[0:rows, c0:c1], scalar=0.0,
                                                       in1=ta_[0:rows, c0:c1], op0=ALU.max, op1=ALU.add).then_inc(
                            count.up(L_raw if c1 > 1024 else dve_steps), 1)
                elif k == "lsplit":
                    h = a[0]
                    hi, lo = Lsp(h)
                    vector.wait_ge(L_hi, h + 1)
                    for rows, c0, c1 in piece_list(h):
                        lower(lo[0:rows, c0:c1], t2(h)[0:rows, c0:c1], hi[0:rows, c0:c1]).then_inc(
                            count.up(L_ready if c1 > 1024 else dve_steps), 1)
                elif k == "wsplit":
                    h = a[0]
                    hi, lo = Wsp(h)
                    vector.wait_ge(W_hi, h + 1)
                    lower(lo[:, 0:ZW], t1(h)[:, 0:ZW], hi[:, 0:ZW]).then_inc(count.up(w_ready), 1)
                elif k == "olow":
                    h = a[0]
                    r = 64 * (h % 2)
                    if h == 0:
                        vector.wait_ge(stored, 16 * 7)
                    vector.wait_ge(o_hi, count.next(o_hi))
                    lower(oT[1][r:r + 64, h // 2, 0:TP], bank(("av", h))[r:r + 64, :],
                          oT[0][r:r + 64, h // 2, 0:TP]).then_inc(count.upto(*read(("av", h))), 1)
                elif k == "sz":
                    vector.wait_ge(brow_in, 16)
                    nc.vector.tensor_copy(brow[:].rearrange("o (b h t) -> o b h t", b=SB, h=H),
                                         sbr[:].unsqueeze(1).unsqueeze(3).to_broadcast([1, SB, H, ST])).then_inc(
                                             count.up(dve_steps), 1)
                    nc.vector.memset(Qb[:], 0.0).then_inc(count.up(dve_steps), 1)
                    vector.wait_ge(*count.last)
                    for h2 in range(2):
                        nc.vector.tensor_copy(Qb[64 * h2:64 * h2 + 64, :, :, 8 * h2:8 * h2 + 8],
                                             qk[64 * h2:64 * h2 + 64, 0, :, TP:T].rearrange("q p (b t) -> q b p t", t=ST)).then_inc(
                                                 count.up(qb_ready), 1)
                elif k == "sav" and a[0] == 3:
                    for h2 in range(2):
                        vector.wait_ge(o_hi, count.next(o_hi))
                        lower(sample_cols(oT[1], h2), sample_out(h2), sample_cols(oT[0], h2)).then_inc(
                            count.upto(*read("sav")) if h2 else count.up(dve_steps), 1)
                elif k == "ysplit":
                    vector.wait_ge(y_hi, count.next(y_hi))
                    lower(yh[1][:], yact[:], yh[0][:]).then_inc(count.up(y_lo), 1)
                elif k == "msinv":
                    w = a[0]
                    if w == 0:
                        for half, ab in enumerate("ab"):
                            vector.wait_ge(*full(("ms", 0, ab)))
                            nc.vector.tensor_scalar(inv[:, HT * half:HT * half + HT], banks[:, half, 0:HT], 1.0 / D, EPS,
                                                       ALU.mult, ALU.add).then_inc(
                                                           count.upto(*read(("ms", 0, ab))), 1)
                        vector.wait_ge(*count.last)
                    else:
                        vector.wait_ge(*read(("ms", 1, "a")))
                        vector.wait_ge(*read(("ms", 1, "b")))
                    nc.vector.reciprocal(inv[:], inv[:]).then_inc(count.up(dve_steps), 1)
                    vector.wait_ge(*count.last)
                elif k == "pT":
                    t = a[0]
                    t0, n = TOK[t]
                    vector.wait_ge(pT_hi, count.next(pT_hi))
                    lower(pT[1][:, :, t0:t0 + n], bank(e)[:, 0:2 * P].rearrange("p (k n) -> p k n", k=2)[:, :, 0:n],
                          pT[0][:, :, t0:t0 + n]).then_inc(count.upto(*read(e)), 1)

        @block.tensor
        def _(tensor):
            count = Count()

            def mm(out, lhsT, rhs, start=False, stop=False):
                return nc.tensor.matmul(out, lhsT, rhs, start=start, stop=stop, skip_group_check=True)

            def three(out, w, x, start=False, stop=False):
                mm(out, w[0], x[0], start=start)
                mm(out, w[0], x[1])
                return mm(out, w[1], x[0], stop=stop)

            def operand(u):
                kind, m0, nk, nm = units[u]
                if kind in ("attn",):
                    return oT
                if kind in ("val", "glu"):
                    return yh
                if kind == "out":
                    return mg
                if kind == "down":
                    return hid[m0 // 8 % 2]
                if kind == "ple":
                    return pT
                return act

            def unit(u):
                kind, m0, nk, nm = units[u]
                tensor.wait_ge(w_lo, u + 1)
                x = operand(u)
                if u == 0:
                    tensor.wait_ge(h_lo, 10)
                if u == FIRST["attn"]:
                    tensor.wait_ge(*read("sav"))
                if u == FIRST["val"]:
                    tensor.wait_ge(y_lo, 1)
                if u == FIRST["ple"]:
                    tensor.wait_ge(*read(("pT", 4)))
                wh, wl = [wview(w, u % NSPLIT, u) for w in (whi, wlo)]
                for j in range(nm):
                    job = ("m", u, j)
                    if used_before(job):
                        tensor.wait_ge(*free(job))
                    out = dplace(job)
                    c = slice(P * j, P * j + P)
                    for k in range(nk):
                        if u == FIRST["out"]:
                            tensor.wait_ge(mg_lo, k + 1)
                        if u == FIRST["up"]:
                            tensor.wait_ge(act_lo, k + 1)
                        if u == FIRST["pgate"]:
                            tensor.wait_ge(act_lo, KT + k + 1)
                        if kind == "down" and j == 0 and m0 % 8 == 0:
                            tensor.wait_ge(hid_lo, 4 * (m0 // 8) + k + 1)
                        for w, xx, first, last in ((wh, x[0], k == 0, False), (wh, x[1], False, False),
                                                   (wl, x[0], False, k == nk - 1)):
                            for half in range(2):
                                ins = mm(out[:, half, 0:HT], w[:, k, c], xx[:, k, HT * half:HT * half + HT],
                                         start=first, stop=last)
                    ins.then_inc(full_of(job), 1)

            def transpose(out, in_, rows=P):
                return nc.tensor.transpose(out, in_, ident[0:rows, 0:rows])

            def page_scores(j):
                b, page = j // NPG, j % NPG
                tensor.wait_ge(*read(("skt", j)))
                for p in range(AT):
                    c = 16 * (AT * b + p)
                    ins = mm(banks[:, page, c:c + 16], KTb[:, j % 2, P * p:P * p + P], Qb[:, b, p, :], stop=True)
                ins.then_inc(kt_used, 1)

            for e in schedule:
                k, a = e[0], e[1:]
                if k == "h":
                    t, half = a
                    n = TOK[t][1]
                    if t == 0 and half == 0:
                        tensor.wait_ge(ident_ready, 1)
                    tensor.wait_ge(xn_ready, t + 1)
                    if used_before(e):
                        tensor.wait_ge(*free(e))
                    for c in range(4):
                        c0 = P * (4 * half + c)
                        ins = transpose(bank(e)[:, P * c:P * c + n], xtok[0:n, t, c0:c0 + P], n)
                    ins.then_inc(full_of(e), 1)
                elif k == "s5ct":
                    tensor.wait_ge(params_in, 16 * N_PARAMS)
                    if used_before(e[0]):
                        tensor.wait_ge(*free(e[0]))
                    for c in range(4):
                        ins = transpose(bank("s5ct")[:, P * c:P * c + P], cnat[:, c // 2, c % 2, :])
                    ins.then_inc(full_of("s5ct"), 1)
                elif k == "s5h0":
                    if used_before("s5h0"):
                        tensor.wait_ge(*free("s5h0"))
                    for c in range(2):
                        ins = transpose(bank("s5h0")[:, P * c:P * c + P], snat[:, c:2 * P:2])
                    ins.then_inc(full_of("s5h0"), 1)
                elif k == "unit":
                    unit(a[0])
                elif k == "qksum":
                    p = a[0]
                    if p == 0:
                        tensor.wait_ge(consts_ready, 1)
                        if used_before("qs0"):
                            tensor.wait_ge(*free("qs0"))
                        if used_before("qs1"):
                            tensor.wait_ge(*free("qs1"))
                    tensor.wait_ge(sq_ready, p + 1)
                    for half in range(2):
                        ins = mm(banks[0:16, half, 0:HT], hsum[:, p, :], gst[:, p % 2, HT * half:HT * half + HT],
                                 start=p == 0, stop=p == 7)
                        if p == 7 and half == 0:
                            ins.then_inc(full_of("qs0"), 1)
                    if p == 7:
                        ins.then_inc(full_of("qs1"), 1)
                    else:
                        ins.then_inc(sq_used, 1)
                elif k == "qknorm":
                    p, half = a
                    if p == 0 and half == 0:
                        tensor.wait_ge(nrm_ready, 1)
                    if used_before(e):
                        tensor.wait_ge(*free(e))
                    mm(bank(e)[:, 0:HT], sel[:, p, :], nrm[:, HT * half:HT * half + HT], True, True).then_inc(
                        full_of(e), 1)
                elif k == "gt":
                    part, n = a
                    tensor.wait_ge(gnat_ready, part + 1)
                    if used_before(e):
                        tensor.wait_ge(*free(e))
                    for c in range(4):
                        ins = transpose(bank(e)[:, P * c:P * c + P],
                                        gnat[:, 4 * n + c].rearrange("q j c -> q (j c)"))
                    ins.then_inc(full_of(e), 1)
                elif k == "vs":
                    tensor.wait_ge(ca_ready, 1)
                    if used_before(e):
                        tensor.wait_ge(*free(e))
                    for c in range(4):
                        g = 8 * (a[0] // 2) + a[0] % 2 + 2 * c
                        r = slice(64 * (g % 2), 64 * (g % 2) + 64)
                        out = bank(e)[0:GC, P * c:P * c + P]
                        for part in range(2):
                            ins = mm(out, bb[r, part, g // 2, :], CA[r, part, g // 2, 0:CH, :].rearrange("q k c -> q (k c)"),
                                     part == 0, part == 1)
                    ins.then_inc(full_of(e), 1)
                elif k in ("kout", "vout"):
                    t = a[0]
                    t0, n = TOK[t]
                    if t == 0:
                        tensor.wait_ge(*read(("qknorm", 7, 1) if k == "kout" else ("m", FIRST["v"] + 3, 0)))
                        tensor.wait_ge(*read(("qknorm", 7, 0) if k == "kout" else ("m", FIRST["v"] + 2, 0)))
                    if used_before(e):
                        tensor.wait_ge(*free(e))
                    for p in range(AT):
                        src = qk[:, 1, p, t0:t0 + n] if k == "kout" else vT[:, p, t0:t0 + n]
                        ins = transpose(bank(e)[0:n, P * p:P * p + P], src)
                    ins.then_inc(full_of(e), 1)
                elif k == "ut":
                    q, half = a
                    tensor.wait_ge(*read(("m", FIRST["u"] + q, 0)))
                    if used_before(e):
                        tensor.wait_ge(*free(e))
                    for c in range(4):
                        j = 4 * half + c
                        ins = transpose(bank(e)[0:NCH, P * c:P * c + P], uT[:, q, j:T:CH])
                    ins.then_inc(full_of(e), 1)
                elif k == "ug":
                    q, half = a
                    for hh in range(2):
                        tensor.wait_ge(*read(("ut", q, hh)))
                    if used_before(e):
                        tensor.wait_ge(*free(e))
                    for c in range(4):
                        src = up_[0:NCH, q % 2, 4 * half + c].rearrange("n j c -> n (j c)")
                        ins = transpose(bank(e)[:, NCH * c:NCH * c + NCH], src, NCH)
                    ins.then_inc(full_of(e), 1)
                elif k == "s":
                    n, part = a
                    if n == 0:
                        for hh in range(2):
                            tensor.wait_ge(*read(("ug", 3, hh)))
                            tensor.wait_ge(*read(("gt", part, 2 + hh)))
                    if used_before(e):
                        tensor.wait_ge(*free(e))
                    for c in range(4):
                        p = 4 * n + c
                        for g2 in range(2):
                            r = slice(64 * g2, 64 * g2 + 64)
                            ins = mm(bank(e)[r, NCH * c:NCH * c + NCH], GT[:, part, p, r], UT[:, 2 * p + g2, :], True, True)
                    ins.then_inc(full_of(e), 1)
                elif k == "sfinal":
                    tensor.wait_ge(fo_ready, 1)
                    if used_before(k):
                        tensor.wait_ge(*free(k))
                    for part in range(2):
                        transpose(banks[:, 0, P * part:P * part + P], Fo[:, part, GP:9 * GP])
                    for part in range(2):
                        ins = transpose(banks[0:GP, 0, P * (2 + part):P * (3 + part)], Fo[:, part, 0:GP])
                    ins.then_inc(full_of(k), 1)
                elif k == "y":
                    q, half = a
                    if q == 0 and half == 0:
                        tensor.wait_ge(t_in, 16 * CH)
                        tensor.wait_ge(scanned, 6)
                    if used_before(e):
                        tensor.wait_ge(*free(e))
                    for c in range(4):
                        g = 8 * q + 2 * c + half
                        r = slice(64 * (g % 2), 64 * (g % 2) + 64)
                        out = bank(e)[0:NCH, P * c:P * c + P]
                        mm(out, UT[:, g, :], Tm[:, g, :], True)
                        for part in range(2):
                            ins = mm(out, Hb[r, part, g // 2, :],
                                     CA[r, part, g // 2, 1:CH + 1, :].rearrange("q k c -> q (k c)"), False, part == 1)
                    ins.then_inc(full_of(e), 1)
                elif k == "yt":
                    q, half = a
                    for hh in range(2):
                        tensor.wait_ge(*read(("y", q, hh)))
                    if used_before(e):
                        tensor.wait_ge(*free(e))
                    for c in range(4):
                        ins = transpose(bank(e)[:, NCH * c:NCH * c + NCH], yb[0:NCH, q % 2, 4 * half + c, :], NCH)
                    ins.then_inc(full_of(e), 1)
                elif k == "z":
                    h = a[0]
                    r = slice(64 * (h % 2), 64 * (h % 2) + 64)
                    if h < 2:
                        for place, n in jobs["z_before", h]:
                            tensor.wait_ge(psum_free[place], n)
                    else:
                        tensor.wait_ge(z_free, h - 1)
                    tensor.wait_ge(qk_lo, 2 * (h // 2) + 2)
                    for b in (0, 1, 3, 2):
                        w = TP - P * b
                        out = zflat(h, P, ZOFF[b], ZOFF[b] + w)
                        ins = three(out, [x[r, P * b:P * b + P] for x in (khi, klo)],
                                    [x[r, P * b:TP] for x in (qhi, qlo)], start=b != 3)
                    ins.then_inc(z_ready, 1)
                elif k == "cum":
                    h = a[0]
                    tensor.wait_ge(L_ready, h + 1)
                    for b in range(4):
                        for c in range(b, 4):
                            w = TP - P * c
                            o0 = ZOFF[b] + P * (c - b)
                            for L in Lsp(h):
                                ins = mm(zflat(h, P, o0, o0 + w), (tri if c == b else negs)[:, :], L[:, ZOFF[c]:ZOFF[c] + w],
                                         stop=True)
                    ins.then_inc(cum_ready, 1)
                elif k == "av":
                    h = a[0]
                    tensor.wait_ge(w_ready, h + 1)
                    tensor.wait_ge(v_lo, h // 2 + 1)
                    if used_before(e):
                        tensor.wait_ge(*free(e))
                    for b in range(4):
                        ins = three(bank(e)[:, P * b:TP], [x[:, P * b:P * b + P] for x in (vhi, vlo)],
                                    [x[:, ZOFF[b]:ZOFF[b] + TP - P * b] for x in Wsp(h)], start=b == 0, stop=b == 3)
                    ins.then_inc(full_of(e), 1)
                elif k == "olow" and a[0] == H - 1:
                    tensor.wait_ge(z_free, H)
                    tensor.wait_ge(*read(("av", H - 1)))
                elif k == "sz":
                    tensor.wait_ge(z_free, H - 1)
                    tensor.wait_ge(qb_ready, 2)
                    for n in range(3):
                        rows = P if n < 2 else ST
                        mm(banks[0:rows, n, :], ones[0:1, 0:rows], brow[:], True)
                    for b in range(SB):
                        for p in range(AT):
                            c = 16 * (AT * b + p)
                            mm(banks[0:ST, 2, c:c + 16], qk[:, 1, p, TP + ST * b:TP + ST * b + ST], Qb[:, b, p, :], stop=True)
                elif k == "skt":
                    j = a[0]
                    tensor.wait_ge(page_in[j % NPAGE], 16 * (j // NPAGE + 1))
                    if used_before(e):
                        tensor.wait_ge(*free(e))
                    for p in range(AT):
                        ins = transpose(dplace(e)[:, 0, P * p:P * p + P], pages[:, j % NPAGE, P * p:P * p + P])
                    ins.then_inc(full_of(e), 1)
                    if j:
                        page_scores(j - 1)
                elif k == "sl":
                    page_scores(SB * NPG - 1)
                elif k == "scum":
                    tensor.wait_ge(L_ready, H + 1)
                    new = slice(1024, SZW)
                    for L in Lsp(H):
                        mm(banks[0:ST, 2, :], tri[0:ST, 0:ST], L[0:ST, new], stop=True)
                        mm(banks[:, 1, :], tri[:, :], L[:, 512:1024])
                        mm(banks[:, 1, :], negs[0:ST, :], L[0:ST, new], stop=True)
                        mm(banks[:, 0, :], tri[:, :], L[:, 0:512])
                        mm(banks[:, 0, :], negs[:, :], L[:, 512:1024])
                        ins = mm(banks[:, 0, :], negs[0:ST, :], L[0:ST, new], stop=True)
                    ins.then_inc(cum_ready, 1)
                elif k == "sav":
                    if a[0] == 0:
                        tensor.wait_ge(w_masked, 4 * H + 1)
                        tensor.wait_ge(z_free, H + 1)
                        if used_before(k):
                            tensor.wait_ge(*free(k))
                    for b in range(2 * a[0], 2 * a[0] + 2):
                        for page in range(NPG):
                            n = SB * NPG + NPG * b + page
                            tensor.wait_ge(page_in[n % NPAGE], 16 * (n // NPAGE + 1))
                        tensor.wait_ge(vnew_in[b], 16)
                        for p in range(AT):
                            c = 16 * (AT * b + p)
                            out = bank(k)[:, c:c + 16]
                            vc = slice(P * p, P * p + P)
                            for page in range(NPG):
                                mm(out, pages[:, (SB * NPG + NPG * b + page) % NPAGE, vc],
                                   t1(H)[:, 512 * page + c:512 * page + c + 16], page == 0)
                            ins = mm(out, vnew[2 * b // SB][:, b % (SB // 2), vc], t1(H)[0:ST, 1024 + c:1024 + c + 16], stop=True)
                        if b < SB - 1:
                            ins.then_inc(vb_used, 1)
                        else:
                            ins.then_inc(full_of(k), 1)
                elif k == "xT":
                    t, half = a
                    n = TOK[t][1]
                    tensor.wait_ge(x2_in[t % 2], 16 * (t // 2 + 1))
                    if used_before(e):
                        tensor.wait_ge(*free(e))
                    for c in range(4):
                        c0 = P * (4 * half + c)
                        ins = transpose(dplace(e)[:, 0, P * c:P * c + n], xtok2[0:n, t % 2, c0:c0 + P], n)
                    ins.then_inc(full_of(e), 1)
                elif k == "ms":
                    w, m = a
                    if m == 0:
                        if used_before(("ms", w, "a")):
                            tensor.wait_ge(*free(("ms", w, "a")))
                        if used_before(("ms", w, "b")):
                            tensor.wait_ge(*free(("ms", w, "b")))
                        if w == 0:
                            tensor.wait_ge(z_free, H + 1)
                    tensor.wait_ge(ms_sq, KT * w + m + 1)
                    for half, ab in enumerate("ab"):
                        ins = mm(banks[:, half, 0:HT], ones[:, :], sq[:, m % 2, HT * half:HT * half + HT], m == 0, m == KT - 1)
                        if m == KT - 1:
                            ins.then_inc(full_of(("ms", w, ab)), 1)
                    if m < KT - 1:
                        ins.then_inc(ms_used, 1)
                elif k == "pT":
                    t = a[0]
                    t0, n = TOK[t]
                    tensor.wait_ge(p_in[t % 2], 16 * (t // 2 + 1))
                    if used_before(e):
                        tensor.wait_ge(*free(e))
                    for c in range(2):
                        ins = transpose(bank(e)[:, P * c:P * c + n], ptok[0:n, t % 2, P * c:P * c + P], n)
                    ins.then_inc(full_of(e), 1)
                elif k == "yout":
                    m = a[0]
                    tensor.wait_ge(yf_ready, m + 1)
                    if used_before(("yout", m, "a")):
                        tensor.wait_ge(*free(("yout", m, "a")))
                    for t in range(4):
                        ins = transpose(banks[:, 2, P * t:P * t + P], yf[:, m % 2, P * t:P * t + P])
                    ins.then_inc(full_of(("yout", m, "a")), 1)
                    if used_before(("yout", m, "b")):
                        tensor.wait_ge(*free(("yout", m, "b")))
                    transpose(banks[0:TS, 3, 0:P], yf[:, m % 2, TP:T]).then_inc(full_of(("yout", m, "b")), 1)


INS = ["x_prompt", "x_sample", "p_prompt", "p_sample", "cache_k", "cache_v", "state_ssm", "page_table",
       "g_mix", "w_in", "g_q", "g_k", "sb_bias", "w_attn_out", "ssm_a_re", "ssm_a_im", "ssm_log_dt",
       "ssm_b_re", "ssm_b_im", "ssm_c_re", "ssm_c_im", "ssm_d", "w_glu_val", "w_glu_gate", "w_out",
       "g_mlp", "w_up", "w_down", "g_ple", "w_ple", "w_ple_gate"]
OUTS = [("y_prompt", (1, TP, D)), ("y_sample", (SB, ST, D)), ("k_prompt", (1, 1, TP, H, HD)),
        ("v_prompt", (1, 1, TP, H, HD)), ("ssm_prompt", (1, 1, G, NS, 2)), ("k_sample", (1, SB, ST, H, HD)),
        ("v_sample", (1, SB, ST, H, HD)), ("ssm_sample", (1, SB, G, NS, 2))]


def kernel(**inputs):
    import concourse.bacc as bacc
    from concourse.bass_utils import run_bass_kernel_spmd as run

    nc = bacc.Bacc("TRN2", target_bir_lowering=False, num_devices=1)
    arrays, i, o = {}, {}, {}
    for name in INS:
        a = np.ascontiguousarray(inputs[name])
        arrays[f"in_{name}"] = a
        i[name] = nc.dram_tensor(f"in_{name}", a.shape, mybir.dt.from_np(a.dtype), kind="ExternalInput").ap()
    for name, shape in OUTS:
        o[name] = nc.dram_tensor(f"out_{name}", shape, F32, kind="ExternalOutput").ap()
    build(nc, i, o)
    r = run(nc, [arrays], core_ids=[0])
    return tuple(r.results[0][f"out_{name}"] for name, _ in OUTS)
```
